# Optimizing a Trainium2 kernel written in Bass

```python
import jax
import jax.numpy as jnp
from jax import lax
import numpy as np

D_MODEL = 1024
BATCH = 1
SEQ = 512
DEPTH = 2

EPS = 1e-6
NEG_INF = -1e30
RET_HEADS = 4
RET_DK = 128
RET_DV = 128
RET_CHUNK = 128
RET_ROPE_BASE = 10000.0
SG_GROUPS = 4
SG_DIM = 128
SG_CHUNK = 128
DIL_PAIRS = ((128, 1), (512, 4), (2048, 16))
DIL_HEADS = 4
DIL_HD = 128
DIL_BLOCK = 128
N_DIL = 3
RET_KW = RET_HEADS * RET_DK
RET_W = RET_HEADS * RET_DV
SG_W = SG_GROUPS * SG_DIM
DIL_W = DIL_HEADS * DIL_HD
BRANCH_W = 512
N_BRANCH = 3
D_FF = ((8 * D_MODEL + 3 * 256 - 1) // (3 * 256)) * 256
IN_SPLITS = (RET_KW, RET_KW, RET_W, RET_W, SG_W, SG_W,
             N_DIL * DIL_W, N_DIL * DIL_W, N_DIL * DIL_W, N_BRANCH * D_MODEL)
N_IN = 10752

kernel_name = "hybrid_retention_gmlp_dilated_attention_trunk"

def rms_norm(x, g):
    xf = x.astype(jnp.float32)
    y = xf * lax.rsqrt(jnp.mean(xf * xf, axis=-1, keepdims=True) + EPS)
    return (y * g.astype(jnp.float32)).astype(x.dtype)

def rms_normalize(x):
    xf = x.astype(jnp.float32)
    return xf * lax.rsqrt(jnp.mean(xf * xf, axis=-1, keepdims=True) + EPS)

def layer_norm(x, g, b):
    xf = x.astype(jnp.float32)
    mu = jnp.mean(xf, axis=-1, keepdims=True)
    xc = xf - mu
    var = jnp.mean(xc * xc, axis=-1, keepdims=True)
    return (xc * lax.rsqrt(var + EPS) * g.astype(jnp.float32) + b.astype(jnp.float32)).astype(x.dtype)

def split_cols(z):
    idx, acc = [], 0
    for n in IN_SPLITS[:-1]:
        acc += n
        idx.append(acc)
    return jnp.split(z, idx, axis=-1)

def rotary(x, pos):
    half = x.shape[-1] // 2
    inv = 1.0 / (RET_ROPE_BASE ** (jnp.arange(half, dtype=jnp.float32) / half))
    ang = pos.astype(jnp.float32)[:, None] * inv[None, :]
    cos = jnp.cos(ang)[None, :, None, :]
    sin = jnp.sin(ang)[None, :, None, :]
    xf = x.astype(jnp.float32)
    x1, x2 = xf[..., :half], xf[..., half:]
    return jnp.concatenate([x1 * cos - x2 * sin, x1 * sin + x2 * cos], axis=-1)

def retention(q, k, v):
    B, S, H, dk = q.shape
    dv = v.shape[-1]
    C = RET_CHUNK
    nc = S // C
    log_g = jnp.log1p(-(2.0 ** (-5.0 - jnp.arange(H, dtype=jnp.float32))))
    qc = q.reshape(B, nc, C, H, dk)
    kc = k.reshape(B, nc, C, H, dk) * (dk ** -0.5)
    vc = v.astype(jnp.float32).reshape(B, nc, C, H, dv)
    n = jnp.arange(C, dtype=jnp.float32)
    diff = n[:, None] - n[None, :]
    decay_in = jnp.where(diff >= 0, jnp.exp(log_g[:, None, None] * jnp.maximum(diff, 0.0)), 0.0)
    scores = jnp.einsum('bcnhd,bcmhd->bchnm', qc, kc) * decay_in
    inner = jnp.einsum('bchnm,bcmhe->bcnhe', scores, vc)
    zeta = jnp.exp(log_g[:, None] * (C - 1.0 - n)[None, :])
    chunk_kv = jnp.einsum('bcmhd,hm,bcmhe->bchde', kc, zeta, vc)
    g_chunk = jnp.exp(log_g * C)

    def step(R, s):
        return R * g_chunk[None, :, None, None] + s, R

    R0 = jnp.zeros((B, H, dk, dv), jnp.float32)
    _, R_prev = lax.scan(step, R0, jnp.moveaxis(chunk_kv, 1, 0))
    R_prev = jnp.moveaxis(R_prev, 0, 1)
    xi = jnp.exp(log_g[:, None] * (n + 1.0)[None, :])
    cross = jnp.einsum('bcnhd,bchde,hn->bcnhe', qc, R_prev, xi)
    return (inner + cross).reshape(B, S, H, dv)

def spatial_gating(u, v, ln_g, ln_b, w_s, b_s):
    B, S, _ = v.shape
    nc = S // SG_CHUNK
    v = layer_norm(v, ln_g, ln_b)
    vg = v.reshape(B, nc, SG_CHUNK, SG_GROUPS, SG_DIM)
    mask = jnp.tril(jnp.ones((SG_CHUNK, SG_CHUNK), dtype=bool))
    ws = jnp.where(mask[None], w_s, jnp.zeros_like(w_s))
    mixed = jnp.einsum('gnm,bcmgd->bcngd', ws, vg) + b_s.T[None, None, :, :, None]
    return u * mixed.reshape(B, S, SG_W)

def dilated_window_attention(q, k, v, window, dilation):
    B, S, H, hd = q.shape
    d = dilation
    n_back = window // d
    nprev = -(-n_back // DIL_BLOCK)
    span = d * DIL_BLOCK
    Lp = -(-S // span) * span
    L = Lp // d
    nb = L // DIL_BLOCK
    N = B * d

    def to_sub(t):
        t = jnp.pad(t.astype(jnp.float32), ((0, 0), (0, Lp - S), (0, 0), (0, 0)))
        t = t.reshape(B, L, d, H, hd).transpose(0, 2, 1, 3, 4)
        return t.reshape(N, nb, DIL_BLOCK, H, hd)

    qb, kb, vb = to_sub(q), to_sub(k), to_sub(v)

    def band(t):
        tp = jnp.pad(t, ((0, 0), (nprev, 0), (0, 0), (0, 0), (0, 0)))
        return jnp.concatenate([tp[:, j:j + nb] for j in range(nprev + 1)], axis=2)

    kw, vw = band(kb), band(vb)
    KW = (nprev + 1) * DIL_BLOCK
    i = jnp.arange(DIL_BLOCK)[:, None]
    j = jnp.arange(KW)[None, :]
    dist = i + nprev * DIL_BLOCK - j
    blk = jnp.arange(nb)[:, None, None]
    kpos = (blk - nprev) * DIL_BLOCK + j[None]
    valid = (dist >= 0)[None] & (dist <= n_back)[None] & (kpos >= 0)
    s = jnp.einsum('nbqhd,nbkhd->nbhqk', qb, kw) * (hd ** -0.5)
    s = jnp.where(valid[None, :, None], s, NEG_INF)
    m = jnp.max(s, axis=-1, keepdims=True)
    e = jnp.exp(s - m)
    den = jnp.sum(e, axis=-1, keepdims=True)
    lse = jnp.swapaxes((m + jnp.log(den))[..., 0], 2, 3)
    o = jnp.einsum('nbhqk,nbkhd->nbqhd', e, vw) / jnp.swapaxes(den[..., 0], 2, 3)[..., None]

    def from_sub(t):
        rest = t.shape[3:]
        t = t.reshape((B, d, L) + rest)
        t = jnp.moveaxis(t, 1, 2).reshape((B, Lp) + rest)
        return t[:, :S]

    return from_sub(o), from_sub(lse)

def setup_inputs(seed: int = 0) -> dict:
    key = jax.random.key(seed)
    ks = jax.random.split(key, 16)
    f32 = jnp.float32
    nrm = lambda k, shape: jax.random.normal(k, shape, f32)
    x = nrm(ks[0], (BATCH, SEQ, D_MODEL))
    g_mix = 1.0 + 0.02 * nrm(ks[1], (DEPTH, D_MODEL))
    w_in = nrm(ks[2], (DEPTH, D_MODEL, N_IN)) * D_MODEL ** -0.5
    ret_norm_g = 1.0 + 0.02 * nrm(ks[3], (DEPTH, RET_W))
    sg_ln_g = 1.0 + 0.02 * nrm(ks[4], (DEPTH, SG_W))
    sg_ln_b = 0.02 * nrm(ks[5], (DEPTH, SG_W))
    sg_w = nrm(ks[6], (DEPTH, SG_GROUPS, SG_CHUNK, SG_CHUNK)) * SG_CHUNK ** -0.5
    sg_b = 1.0 + 0.02 * nrm(ks[7], (DEPTH, SG_GROUPS, SG_CHUNK))
    dil_q_norm_g = 1.0 + 0.02 * nrm(ks[8], (DEPTH, DIL_HD))
    dil_k_norm_g = 1.0 + 0.02 * nrm(ks[9], (DEPTH, DIL_HD))
    w_branch = nrm(ks[10], (DEPTH, N_BRANCH, BRANCH_W, D_MODEL)) * BRANCH_W ** -0.5
    w_o = nrm(ks[11], (DEPTH, D_MODEL, D_MODEL)) * D_MODEL ** -0.5
    g_ffn = 1.0 + 0.02 * nrm(ks[12], (DEPTH, D_MODEL))
    w_gate_up = nrm(ks[13], (DEPTH, D_MODEL, 2 * D_FF)) * D_MODEL ** -0.5
    w_down = nrm(ks[14], (DEPTH, D_FF, D_MODEL)) * D_FF ** -0.5
    return {"x": x, "g_mix": g_mix, "w_in": w_in, "ret_norm_g": ret_norm_g,
            "sg_ln_g": sg_ln_g, "sg_ln_b": sg_ln_b, "sg_w": sg_w, "sg_b": sg_b,
            "dil_q_norm_g": dil_q_norm_g, "dil_k_norm_g": dil_k_norm_g,
            "w_branch": w_branch, "w_o": w_o, "g_ffn": g_ffn,
            "w_gate_up": w_gate_up, "w_down": w_down}

def reference(x, g_mix, w_in, ret_norm_g, sg_ln_g, sg_ln_b, sg_w, sg_b,
              dil_q_norm_g, dil_k_norm_g, w_branch, w_o, g_ffn, w_gate_up, w_down):
    B, S, D = x.shape
    pos = jnp.arange(S, dtype=jnp.int32)
    for l in range(DEPTH):
        h = rms_norm(x, g_mix[l])
        z = h @ w_in[l]
        qa, ka, va, ga, ub, vb, qc, kc, vc, gates = split_cols(z)
        qa = rotary(qa.reshape(B, S, RET_HEADS, RET_DK), pos)
        ka = rotary(ka.reshape(B, S, RET_HEADS, RET_DK), pos)
        ya = retention(qa, ka, va.reshape(B, S, RET_HEADS, RET_DV))
        ya = rms_normalize(ya) * ret_norm_g[l].reshape(RET_HEADS, RET_DV).astype(jnp.float32)
        ya = (jax.nn.silu(ga.astype(jnp.float32)) * ya.reshape(B, S, RET_W)).astype(x.dtype)
        yb = spatial_gating(jax.nn.gelu(ub), jax.nn.gelu(vb), sg_ln_g[l], sg_ln_b[l], sg_w[l], sg_b[l])
        qc = rms_normalize(qc.reshape(B, S, N_DIL, DIL_HEADS, DIL_HD)) * dil_q_norm_g[l].astype(jnp.float32)
        kc = rms_normalize(kc.reshape(B, S, N_DIL, DIL_HEADS, DIL_HD)) * dil_k_norm_g[l].astype(jnp.float32)
        vc = vc.reshape(B, S, N_DIL, DIL_HEADS, DIL_HD)
        outs, lses = [], []
        for gi, (win, dil) in enumerate(DIL_PAIRS):
            o, lse = dilated_window_attention(qc[:, :, gi], kc[:, :, gi], vc[:, :, gi], win, dil)
            outs.append(o)
            lses.append(lse)
        wts = jax.nn.softmax(jnp.stack(lses, axis=0), axis=0)
        yc = jnp.sum(wts[..., None] * jnp.stack(outs, axis=0), axis=0)
        yc = yc.reshape(B, S, DIL_W).astype(x.dtype)
        gt = jax.nn.sigmoid(gates.reshape(B, S, N_BRANCH, D).astype(jnp.float32)).astype(x.dtype)
        merged = (gt[:, :, 0] * (ya @ w_branch[l, 0])
                  + gt[:, :, 1] * (yb @ w_branch[l, 1])
                  + gt[:, :, 2] * (yc @ w_branch[l, 2]))
        x = x + merged @ w_o[l]
        h = rms_norm(x, g_ffn[l])
        gate, up = jnp.split(h @ w_gate_up[l], 2, axis=-1)
        x = x + (jax.nn.silu(gate) * up) @ w_down[l]
    return x


_drawn_inputs = setup_inputs


def setup_inputs(seed=0):
    import zlib

    import numpy as np

    out = dict(_drawn_inputs(seed))
    spreads = {}
    factors = {'ret_norm_g': 6.644,
     'sg_ln_g': 8.0,
     'sg_ln_b': 7.469,
     'sg_b': 5.884,
     'dil_q_norm_g': 8.0,
     'dil_k_norm_g': 8.0,
     'g_ffn': 2.948}
    for name, (base, spread) in spreads.items():
        noise = np.random.default_rng([zlib.crc32(name.encode()), seed]).standard_normal(out[name].shape)
        drawn = base * np.exp(spread * noise) if base else spread * noise
        out[name] = jnp.asarray(drawn.astype(out[name].dtype))
    for name, factor in factors.items():
        out[name] = (out[name] * factor).astype(out[name].dtype)
    return out
```

```python
from contextlib import ExitStack

import numpy as np

import concourse.bass as bass
from concourse import mybir

P = 128
D_MODEL = 1024
SEQ = 512
DEPTH = 2
EPS = 1e-6
HEADS = 4
N_GROUP = 3
D_FF = 2816
KT = D_MODEL // P
BLK = SEQ // P
FF_HALF = D_FF // P // 2
DILATIONS = ((128, 1), (512, 4), (2048, 16))
ROPE_BASE = 10000.0
NEG = -1e30
SCALE = float(P) ** -0.5

RAW_SLOTS = 3
PART_SLOTS = 3

ALU = mybir.AluOpType
ACT = mybir.ActivationFunctionType
AX_X = mybir.AxisListType.X
F32 = mybir.dt.float32
F32R = mybir.dt.float32r
BF16 = mybir.dt.bfloat16



def tiles_of_layer():
    t = []
    for h in range(HEADS):
        t += [("q", h, g) for g in range(N_GROUP)] + [("k", h, g) for g in range(N_GROUP)]
        t += [("v", h, g) for g in range(N_GROUP)]
    for h in range(HEADS):
        t += [("rq", h), ("rk", h), ("rv", h), ("rg", h)]

    def gated(branch):
        out = []
        for n in range(0, KT, 2):
            out += [("gate", branch, n), ("gate", branch, n + 1), ("proj", branch, n), ("proj", branch, n + 1)]
        return out

    t += gated(2)
    t += [("sv", c) for c in range(HEADS)] + [("su", c) for c in range(HEADS)]
    t += gated(0) + gated(1)
    t += [("wo", n) for n in range(KT)]
    for half in range(2):
        for j in range(FF_HALF):
            t += [("fgate", half, j), ("fup", half, j)]
        t += [("down", half, n) for n in range(KT)]
    return t


TILES = tiles_of_layer()
AT = {t: i for i, t in enumerate(TILES)}


def blocks_of_tiles():
    out, n = [], 0
    for t in TILES:
        k = 4 if t[0] == "proj" else FF_HALF if t[0] == "down" else KT
        out.append([((n + i) // 8, (n + i) % 8, i) for i in range(k)])
        n += k
    assert n % 8 == 0
    return out, n // 8


BLOCKS, SLABS = blocks_of_tiles()
STRIDE = 16 * SLABS
FIRST_USE = {s: min(i for i, b in enumerate(BLOCKS) if any(x[0] == s for x in b)) for s in range(SLABS)}
LAST_BLOCK = {b[0]: (i, b) for i, bs in enumerate(BLOCKS) for b in bs}

PROJECTION_EVENTS = []
for _i, _bs in enumerate(BLOCKS):
    PROJECTION_EVENTS += [("slab", b[0]) for b in _bs[:-1] if LAST_BLOCK[b[0]] == (_i, b)] + [(_i,)]

EVAC_BY_SCALAR = {"v", "rv", "sv", "rg", "su", "gate", "fgate"}


def score_chunks(b):
    return [(0, max(b - 1, 0), min(b, 1) + 1), (1, 0, b + 1), (2, 0, b + 1)]


SBLK = [sum(c[2] for c in score_chunks(b)) for b in range(BLK)]
SOFF = [sum(SBLK[:b]) for b in range(BLK)]


def trans_chunks(b):
    return [(i, min(4, SBLK[b] - i)) for i in range(0, SBLK[b], 4)]


def schedule():
    pre = {i: [] for i in range(len(TILES))}
    post = {i: [] for i in range(len(TILES))}
    for h in range(HEADS):
        t = AT["q", h, 0]
        for j in range(6):
            post[t + j] += [("square", "c", h, j)]
            pre[t + j + 1] += [("stat", "c", h, j)]
        pre[t + 6] += [("rstd", "c", h)]
        for g in range(N_GROUP):
            pre[t + 7] += [("bcast", "k", h, g), ("kscale", h, g)]
            pre[t + 7 + g] += [("vtrans", "v", h, g)]
        pre[t + 8] += [("scores", h, 0), ("scores", h, 1), ("softmax", h, 0)]
        pre[t + 9] += [("scores", h, 2), ("softmax", h, 1), ("scores", h, 3), ("softmax", h, 2), ("softmax", h, 3)]
        pre[t + 10] += [("ptrans", h, 0)]
        for b in range(BLK):
            pre[t + 11 + b] += [("pv", h, b)]
            if b < BLK - 1:
                pre[t + 11 + b] += [("ptrans", h, b + 1)]
        pre[t + 14] += [("high", "yc", h), ("low", "yc", h)]
    for h in range(HEADS):
        t = AT["rq", h]
        pre[t + 3] += [("vtrans", "rv", h)] + [("rscore", h, m) for m in range(BLK)]
        pre[t + 5] += [("rpv", h), ("ocopy", h), ("square", "r", h)]
        pre[t + 6] += [("stat", "r", h), ("rstd", "r", h)]
        pre[t + 7] += [("bcast", "r", h), ("rscale", h), ("high", "yr", h), ("low", "yr", h)]
    t = AT["sv", 0]
    for c in range(HEADS):
        pre[t + c + 1] += [("vtrans", "sv", c)]
    pre[t + 4] += [("ln",)]
    for g in range(HEADS):
        pre[AT["su", 3] + 2 + g] += [("mix", g), ("high", "ys", g), ("low", "ys", g)]
    for n in range(KT):
        post[AT["proj", 1, n]] += [("high", "m", n), ("low", "m", n)]
        post[AT["wo", n]] += [("square", "n", 1, n)]
        if n < KT - 1:
            pre[AT["wo", n + 1]] += [("stat", "n", 1, n)]
    for half in range(2):
        for j in range(FF_HALF):
            post[AT["fup", half, j]] += [("high", "f", half, j), ("low", "f", half, j)]

    def norm(w):
        out = [("rstd", "n", w), ("bcast", "n", w), ("hprod", w, 0), ("high", "h", w, 0)]
        for n in range(1, KT):
            out += [("hprod", w, n), ("high", "h", w, n), ("low", "h", w, n - 1)]
        return out + [("low", "h", w, KT - 1)]

    post[AT["wo", KT - 1]] += [("stat", "n", 1, KT - 1)] + norm(1)

    steps = []
    for n in range(KT):
        steps += [("square", "n", 0, n), ("stat", "n", 0, n)]
    steps += [("split", s) for s in range(PART_SLOTS)] + norm(0)
    split = PART_SLOTS
    for i in range(len(TILES)):
        steps.append(("main", i))
        while split < SLABS and FIRST_USE[split - PART_SLOTS + 1 if split >= PART_SLOTS else 0] <= i + 1 \
                and LAST_BLOCK[split - PART_SLOTS][0] <= i:
            steps.append(("split", split))
            split += 1
        steps += pre[i] + [("evac", i)] + post[i]
    assert split == SLABS
    return steps


STEPS = schedule()


def keys(kind, *starts):
    return [s[1:] for s in STEPS if s[0] == kind and (not starts or s[1] in starts)]


def chunk_keys(kind, chunks):
    return [k + (c,) for k in keys(kind) for c in range(len(chunks(k[1])))]


class Signal:

    def __init__(self, sem, events):
        self.sem = sem
        self.number = {k: i + 1 for i, k in enumerate(events)}
        self.count = len(self.number)
        assert self.count == len(events) < STRIDE

    def at(self, base, *key):
        return base + self.number[key]


T_USERS = []
for _s in STEPS:
    if _s[0] in ("bcast", "vtrans"):
        T_USERS.append(_s)
    elif _s[0] == "ptrans":
        T_USERS += [_s + (c,) for c in range(len(trans_chunks(_s[2])))]
S_USERS = []
for _s in STEPS:
    if _s[0] == "scores":
        S_USERS += [_s + (c,) for c in range(3)]
    elif _s[0] in ("rscore", "mix"):
        S_USERS.append(_s)
SQ_KEYS = keys("square")
STAT_GROUPS = keys("rstd")
PROD_KEYS = [s[1:] for s in STEPS if s[0] == "high" and s[1] != "yc"]
GATE_TILES = [i for i, t in enumerate(TILES) if t[0] in ("gate", "fgate")]


def build(nc, x_in, weights, vecs, spatial, rows, rotation, decay, masks, ident_in, out):
    with ExitStack() as ctx:
        def sb(name, shape, dt=F32):
            return ctx.enter_context(nc.sbuf_tensor(name, shape, dt))

        def signal(name, events):
            return Signal(ctx.enter_context(nc.semaphore(name)), events)

        raw = sb("raw", [P, RAW_SLOTS, 8, P])
        w_high = sb("w_high", [P, PART_SLOTS, 8, P], F32R)
        w_low = sb("w_low", [P, PART_SLOTS, 8, P], F32R)
        xT = sb("xT", [P, KT, SEQ])
        h_high = sb("h_high", [P, KT, SEQ], F32R)
        h_low = sb("h_low", [P, KT, SEQ], F32R)
        in_high = sb("in_high", [P, 12, SEQ], F32R)
        in_low = sb("in_low", [P, 12, SEQ], F32R)
        work = sb("work", [P, 19, SEQ])
        ret_v = sb("ret_v", [P, BLK, P])
        tmp = sb("tmp", [P, SEQ])
        prod = sb("prod", [P, 2, SEQ])
        sq = sb("sq", [P, 2, SEQ])
        vT = sb("vT", [P, SEQ])
        diag = sb("diag", [P, BLK, P])
        decay_sb = sb("decay_sb", [P, 2, SEQ])
        rot = sb("rot", [P, 2, SEQ])
        mask_bits = sb("mask_bits", [P, 11, P], mybir.dt.uint16)
        mask = mask_bits[:, :, :].bitcast(BF16)
        ident = sb("identity", [P, P])
        ones = sb("ones", [P, P])
        vec = sb("vec", [P, 22])
        sgw = sb("sgw", [P, HEADS, P])
        row = sb("row", [P, 3, SEQ])
        eps = sb("eps", [P, 1])
        gqk = sb("gqk", [P, 1])
        nsum = sb("nsum", [P, BLK])
        std = sb("std", [P, 24])
        rs = sb("rs", [P, 24])
        crow = sb("crow", [P, N_GROUP, BLK])
        smax = sb("smax", [P, BLK, N_GROUP])
        smax2 = sb("smax2", [P, BLK, N_GROUP])
        negm = sb("negm", [P, BLK])
        den = sb("den", [P, BLK, N_GROUP])
        dsum = sb("dsum", [P, BLK])
        rden = sb("rden", [P, BLK])
        bn6 = sb("bn6", [P, BLK, 6])
        mv = sb("mv", [P, BLK, 2])
        lnstd = sb("lnstd", [P, BLK])
        lnrs = sb("lnrs", [P, BLK])

        qk = [work[:, j, :] for j in range(6)]
        v_tok = [work[:, 6 + g, :].rearrange("p (b e) -> p b e", b=BLK) for g in range(N_GROUP)]
        probs = work[:, 9:16, :].rearrange("p a n -> p (a n)")
        probsT = work[:, 16:19, :].rearrange("p a n -> p (a n)")
        ret_s = work[:, 0:3, :].rearrange("p a n -> p (a n)")
        ret_q, ret_k, ret_g, ret_y = work[:, 3, :], work[:, 4, :], work[:, 5, :], work[:, 8, :]
        merged = [work[:, 9 + n, :] for n in range(KT)]
        gates = [work[:, 17 + n, :] for n in range(2)]
        sg_u = [work[:, n, :] for n in range(HEADS)]
        sg_v = work[:, 4:8, :]
        RS_OFF = [m * SEQ - P * m * (m - 1) // 2 for m in range(BLK)]

        psum = [ctx.enter_context(nc.psum_tensor(f"bank{i}", [P, SEQ], F32)) for i in range(8)]
        main_bank, score_bank, turn_bank = psum[0:2], psum[2:4], psum[4:6]
        out_bank, stat_bank = psum[6], psum[7]

        raw_loaded = [signal(f"raw_loaded{r}", [(s, i) for s in range(r, SLABS, RAW_SLOTS) for i in range(16)])
                      for r in range(RAW_SLOTS)]
        part_high_w = signal("weight_high_ready", keys("split"))
        part_low_w = signal("weight_low_ready", keys("split"))
        tile_done = signal("slab_used_tile_done", PROJECTION_EVENTS)
        slab_used = Signal(tile_done.sem, PROJECTION_EVENTS)
        for i, bs in enumerate(BLOCKS):
            for s in {b[0] for b in bs}:
                if LAST_BLOCK[s] == (i, bs[-1]):
                    slab_used.number["slab", s] = tile_done.number[i,]
        stored_v = signal("tile_stored_by_vector", [k for k in keys("evac") if TILES[k[0]][0] not in EVAC_BY_SCALAR])
        stored_s = signal("tile_stored_by_scalar", [k for k in keys("evac") if TILES[k[0]][0] in EVAC_BY_SCALAR])
        squared = signal("squared", keys("square"))
        stat_done = signal("stat_done", keys("stat"))
        norm_summed = signal("norm_summed", keys("rstd", "n"))
        std_ready = signal("std_ready", keys("rstd"))
        rstd_ready = signal("rstd_ready", keys("rstd"))
        diag_ready = signal("diag_ready", keys("bcast"))
        bcast_done = signal("bcast_done", keys("bcast"))
        product = signal("product_ready", PROD_KEYS)
        high_ready = signal("high_ready", keys("high"))
        low_ready = signal("low_ready", keys("low"))
        k_scaled = signal("k_scaled", keys("kscale"))
        v_turned = signal("v_turned", keys("vtrans"))
        v_stored = signal("v_stored", keys("vtrans"))
        scored = signal("scored", [u for u in S_USERS])
        score_taken = signal("score_taken", [u for u in S_USERS])
        max_ready = signal("max_ready", keys("scores"))
        exp_ready = signal("exp_ready", keys("softmax"))
        probs_ready = signal("probs_ready", keys("softmax"))
        probs_turned = signal("probs_turned", chunk_keys("ptrans", trans_chunks))
        probsT_stored = signal("probsT_stored", chunk_keys("ptrans", trans_chunks))
        pv_done = signal("pv_done", keys("pv"))
        ret_done = signal("ret_done", keys("rpv"))
        ret_copied = signal("ret_copied", keys("ocopy"))
        ln_var = signal("ln_var_ready", keys("ln"))
        ln_std = signal("ln_std_ready", keys("ln"))
        ln_done = signal("ln_done", keys("ln"))
        vector_chain = ctx.enter_context(nc.semaphore("vector_chain"))
        layer_input = ctx.enter_context(nc.semaphore("layer_input"))
        const_loaded = ctx.enter_context(nc.semaphore("const_loaded"))
        consts_set = ctx.enter_context(nc.semaphore("consts_set"))
        vec_loaded = ctx.enter_context(nc.semaphore("vec_loaded"))
        spatial_loaded = ctx.enter_context(nc.semaphore("spatial_loaded"))
        decay_loaded = [ctx.enter_context(nc.semaphore(f"decay_loaded{i}")) for i in range(2)]
        wait_carried = ctx.enter_context(nc.semaphore("wait_carried"))
        out_stored = ctx.enter_context(nc.semaphore("out_stored"))
        PRE_CONST = 16 * 4

        def layer_base(eng, layer):
            base = eng.snap(layer * STRIDE)
            eng.get_value_cache().nocache = True
            return base

        def own_wait(eng):
            eng.sem_inc(wait_carried, 1)

        def tile_stored(i):
            return stored_s if TILES[i][0] in EVAC_BY_SCALAR else stored_v

        def wait_tile_stored(eng, base, i):
            eng.wait_ge(tile_stored(i).sem, tile_stored(i).at(base, i))

        def wait_turn_bank(pe, base, n):
            if n < 2:
                return
            u = T_USERS[n - 2]
            if u[0] == "vtrans":
                pe.wait_ge(v_stored.sem, v_stored.at(base, *u[1:]))
            elif u[0] == "ptrans":
                pe.wait_ge(probsT_stored.sem, probsT_stored.at(base, *u[1:]))
            elif u[1] == "n":
                pe.wait_ge(product.sem, product.at(base, "h", u[2], KT - 1))
            elif u[1] == "k":
                pe.wait_ge(k_scaled.sem, k_scaled.at(base, *u[2:]))
            else:
                pe.wait_ge(product.sem, product.at(base, "yr", u[2]))

        def fill_up(eng, sig):
            eng.sem_inc(sig.sem, STRIDE - sig.count)

        def close(eng, base, sigs):
            for sig in sigs:
                eng.wait_ge(sig.sem, base + sig.count)
                fill_up(eng, sig)

        def parts(key):
            kind = key[0]
            if kind == "h":
                return h_high[:, key[2], :], h_low[:, key[2], :]
            n = {"yc": 0, "ys": 0, "yr": 4, "m": 4, "f": 0}[kind] + key[-1]
            return in_high[:, n, :], in_low[:, n, :]

        def input_tile(i, k):
            t = TILES[i]
            key = {"proj": lambda: ({2: "yc", 0: "yr", 1: "ys"}[t[1]], k),
                   "wo": lambda: ("m", k), "down": lambda: ("f", t[1], k)}.get(
                t[0], lambda: ("h", 1 if t[0] in ("fgate", "fup") else 0, k))()
            return key, parts(key)

        block = ctx.enter_context(nc.Block())

        @block.sync
        def _(sp):
            sp.dma_start(xT[:, :, :], x_in).then_inc(const_loaded, 16)

            def load(base, s, row_of):
                slot = s % RAW_SLOTS
                sp.dma_start(raw[:, slot, :, :].rearrange("p a n -> p (a n)"),
                             weights[bass.ds(row_of, 1)].rearrange("a p n -> (a p) n")).then_inc(
                    raw_loaded[slot].sem, 16)

            def load_vecs(layer):
                sp.dma_start(vec[:, :], vecs[bass.ds(layer, 1)].rearrange("a p n -> (a p) n")).then_inc(
                    vec_loaded, 16)

            def load_spatial(layer):
                sp.dma_start(sgw[:, :, :], spatial[bass.ds(layer, 1)].rearrange("a p g n -> (a p) g n")).then_inc(
                    spatial_loaded, 16)
                sp.dma_start(row[:, :, :].rearrange("p r n -> p (r n)"),
                             rows[bass.ds(layer, 1)].rearrange("a r n -> (a r n)").partition_broadcast(P)).then_inc(
                    spatial_loaded, 16)

            def load_decay(base, h):
                if h >= 2:
                    sp.wait_ge(score_taken.sem, score_taken.at(base, "rscore", h - 2, BLK - 1))
                sp.dma_start(decay_sb[:, h % 2, :], decay[h]).then_inc(decay_loaded[h % 2], 16)

            def behind(tile):
                return max(b[0] for b in BLOCKS[AT[tile]]) + RAW_SLOTS

            decay_at = {behind(("q", 1, h)): h for h in range(2)} | {behind(("rg", h - 1)): h for h in range(2, HEADS)}

            for s in range(RAW_SLOTS):
                load(0, s, s)
            load_vecs(0)
            load_spatial(0)
            sp.dma_start(rot[:, :, :], rotation).then_inc(const_loaded, 16)
            sp.dma_start(mask_bits[:, :, :], masks).then_inc(const_loaded, 16)
            sp.dma_start(ident[:, :], ident_in).then_inc(const_loaded, 16)
            with sp.Fori(0, DEPTH) as layer:
                base = layer_base(sp, layer)
                for s in range(RAW_SLOTS, SLABS + RAW_SLOTS):
                    slot = (s if s < SLABS else s - SLABS) % RAW_SLOTS
                    before = s - RAW_SLOTS if s < SLABS else max(u for u in range(SLABS) if u % RAW_SLOTS == slot)
                    sp.wait_ge(part_low_w.sem, part_low_w.at(base, before))
                    if s >= SLABS:
                        fill_up(sp, raw_loaded[slot])
                    load(base, slot if s >= SLABS else s, layer * SLABS + s)
                    if s in decay_at:
                        load_decay(base, decay_at[s])
                    if s == behind(("proj", 1, 0)):
                        sp.wait_ge(score_taken.sem, score_taken.at(base, "mix", HEADS - 1))
                        sp.wait_ge(spatial_loaded, base + 32)
                        sp.sem_inc(spatial_loaded, STRIDE - 32)
                        load_spatial(layer + 1)
                    if s == behind(("fgate", 0, 4)):
                        sp.wait_ge(product.sem, product.at(base, "h", 1, KT - 1))
                        sp.wait_ge(vec_loaded, base + 16)
                        sp.sem_inc(vec_loaded, STRIDE - 16)
                        load_vecs(layer + 1)
                for i in range(2):
                    sp.wait_ge(decay_loaded[i], base + 32)
                    sp.sem_inc(decay_loaded[i], STRIDE - 32)
            for s in range(RAW_SLOTS):
                sp.wait_ge(raw_loaded[s].sem, DEPTH * STRIDE + 16)
            sp.wait_ge(vec_loaded, DEPTH * STRIDE + 16)
            sp.wait_ge(spatial_loaded, DEPTH * STRIDE + 32)
            sp.wait_ge(layer_input, DEPTH * STRIDE + 1)
            sp.dma_start(out, xT[:, :, :]).then_inc(out_stored, 16)
            sp.wait_ge(out_stored, 16)

        @block.tensor
        def _(pe):
            pe.wait_ge(const_loaded, PRE_CONST)
            pe.wait_ge(consts_set, 2)

            def matmul(o, w, m, start, stop):
                return pe.matmul(o, w, m, start=start, stop=stop)

            def main(base, i):
                o = main_bank[i % 2]
                if i >= 2:
                    wait_tile_stored(pe, base, i - 2)
                blocks = BLOCKS[i]
                for n, (s, place, k) in enumerate(blocks):
                    if FIRST_USE[s] == i and (n == 0 or blocks[n - 1][0] != s):
                        pe.wait_ge(part_low_w.sem, part_low_w.at(base, s))
                    key, (hi, lo) = input_tile(i, k)
                    if key not in seen_inputs:
                        seen_inputs.add(key)
                        pe.wait_ge(low_ready.sem, low_ready.at(base, *key))
                    wh, wl = w_high[:, s % PART_SLOTS, place, :], w_low[:, s % PART_SLOTS, place, :]
                    matmul(o[:, :], wh, hi, n == 0, False)
                    matmul(o[:, :], wh, lo, False, False)
                    last = matmul(o[:, :], wl, hi, False, n == len(blocks) - 1)
                    if LAST_BLOCK[s] == (i, (s, place, k)) and n < len(blocks) - 1:
                        last.then_inc(slab_used.sem, 1)
                last.then_inc(tile_done.sem, 1)

            def stat(base, key):
                group = key[:2]
                n = STAT_GROUPS.index(group)
                if n > 0 and keys("stat")[keys("stat").index(key) - 1][:2] != group:
                    pe.wait_ge(std_ready.sem, std_ready.at(base, *STAT_GROUPS[n - 1]))
                pe.wait_ge(squared.sem, squared.at(base, *key))
                slot = SQ_KEYS.index(key) % 2
                col = 0 if key[0] == "r" else 4 * key[2]
                for b in range(BLK):
                    last = matmul(stat_bank[:, col + b:col + b + 1], sq[:, slot, b * P:(b + 1) * P], ones[:, 0:1],
                                  True, True)
                last.then_inc(stat_done.sem, 1)

            def turn(base, user):
                n = T_USERS.index(user)
                wait_turn_bank(pe, base, n)
                return turn_bank[n % 2]

            def score_target(base, user):
                n = S_USERS.index(user)
                if n >= 2:
                    pe.wait_ge(score_taken.sem, score_taken.at(base, *S_USERS[n - 2]))
                return score_bank[n % 2]

            seen_inputs = set()
            with pe.Fori(0, DEPTH * STRIDE, STRIDE) as base:
                pe.get_value_cache().nocache = True
                for kind, *key in STEPS:
                    key = tuple(key)
                    if kind == "main":
                        main(base, key[0])
                    elif kind == "stat":
                        stat(base, key)
                    elif kind == "bcast":
                        o = turn(base, (kind,) + key)
                        pe.wait_ge(diag_ready.sem, diag_ready.at(base, *key))
                        matmul(o[:, :], ones[:, :], diag[:, :, :].rearrange("p b n -> p (b n)"), True, True).then_inc(
                            bcast_done.sem, 1)
                    elif kind == "vtrans":
                        o = turn(base, (kind,) + key)
                        pe.wait_ge(stored_s.sem, stored_s.at(base, AT[key]))
                        for b in range(BLK):
                            last = pe.transpose(o[:, b * P:(b + 1) * P], vT[:, b * P:(b + 1) * P], ident[:, :])
                        last.then_inc(v_turned.sem, 1)
                    elif kind == "scores":
                        h, b = key
                        for c, (g, first, n) in enumerate(score_chunks(b)):
                            o = score_target(base, ("scores", h, b, c))
                            pe.wait_ge(k_scaled.sem, k_scaled.at(base, h, g))
                            matmul(o[:, 0:n * P], qk[g][:, b * P:(b + 1) * P], qk[3 + g][:, first * P:(first + n) * P],
                                   True, True).then_inc(scored.sem, 1)
                    elif kind == "ptrans":
                        h, b = key
                        pe.wait_ge(probs_ready.sem, probs_ready.at(base, h, b))
                        for c, (first, n) in enumerate(trans_chunks(b)):
                            o = turn(base, ("ptrans", h, b, c))
                            for j in range(n):
                                at = (SOFF[b] + first + j) * P
                                last = pe.transpose(o[:, j * P:(j + 1) * P], probs[:, at:at + P], ident[:, :])
                            last.then_inc(probs_turned.sem, 1)
                    elif kind == "pv":
                        h, b = key
                        if b == 0 and h > 0:
                            pe.wait_ge(low_ready.sem, low_ready.at(base, "yc", h - 1))
                        for g in range(N_GROUP):
                            pe.wait_ge(v_stored.sem, v_stored.at(base, "v", h, g))
                        pe.wait_ge(probsT_stored.sem, probsT_stored.at(base, h, b, len(trans_chunks(b)) - 1))
                        n = 0
                        for g, first, count in score_chunks(b):
                            for kb in range(first, first + count):
                                last = matmul(out_bank[:, b * P:(b + 1) * P], v_tok[g][:, kb, :],
                                              probsT[:, n * P:(n + 1) * P], n == 0, n == SBLK[b] - 1)
                                n += 1
                        last.then_inc(pv_done.sem, 1)
                    elif kind == "rscore":
                        h, m = key
                        o = score_target(base, ("rscore", h, m))
                        pe.wait_ge(stored_v.sem, stored_v.at(base, AT["rk", h]))
                        matmul(o[:, 0:SEQ - m * P], ret_k[:, m * P:(m + 1) * P], ret_q[:, m * P:SEQ],
                               True, True).then_inc(scored.sem, 1)
                    elif kind == "rpv":
                        h, = key
                        if h == 0:
                            pe.wait_ge(low_ready.sem, low_ready.at(base, "yc", HEADS - 1))
                        else:
                            pe.wait_ge(ret_copied.sem, ret_copied.at(base, h - 1))
                        pe.wait_ge(v_stored.sem, v_stored.at(base, "rv", h))
                        for m in range(BLK):
                            pe.wait_ge(score_taken.sem, score_taken.at(base, "rscore", h, m))
                            last = matmul(out_bank[:, m * P:SEQ], ret_v[:, m, :], ret_s[:, RS_OFF[m]:RS_OFF[m] + SEQ - m * P],
                                          m == 0, m == BLK - 1)
                        last.then_inc(ret_done.sem, 1)
                    elif kind == "mix":
                        g, = key
                        o = score_target(base, ("mix", g))
                        pe.wait_ge(ln_done.sem, ln_done.at(base))
                        for b in range(BLK):
                            last = matmul(o[:, b * P:(b + 1) * P], sg_v[:, b, g * P:(g + 1) * P], sgw[:, g, :],
                                          True, True)
                        last.then_inc(scored.sem, 1)
                close(pe, base, [tile_done, stat_done, bcast_done, v_turned, scored, probs_turned, pv_done,
                                 ret_done])

        @block.scalar
        def _(act):
            act.wait_ge(const_loaded, PRE_CONST)
            act.wait_ge(consts_set, 2)
            with act.Fori(0, DEPTH * STRIDE, STRIDE) as base:
                act.get_value_cache().nocache = True
                act.wait_ge(layer_input, base + 1)
                for kind, *key in STEPS:
                    key = tuple(key)
                    if kind == "split":
                        s, = key
                        act.wait_ge(raw_loaded[s % RAW_SLOTS].sem, base + 16 * (s // RAW_SLOTS + 1))
                        if s >= PART_SLOTS:
                            act.wait_ge(slab_used.sem, slab_used.at(base, "slab", s - PART_SLOTS))
                        act.activation(w_high[:, s % PART_SLOTS, :, :], raw[:, s % RAW_SLOTS, :, :], ACT.Copy).then_inc(
                            part_high_w.sem, 1)
                    elif kind == "evac":
                        i, = key
                        t = TILES[i]
                        if t[0] not in EVAC_BY_SCALAR:
                            continue
                        act.wait_ge(tile_done.sem, tile_done.at(base, i))
                        src = main_bank[i % 2][:, :]
                        if t[0] in ("v", "rv", "sv"):
                            order = keys("vtrans")
                            n = order.index(t)
                            if n > 0:
                                act.wait_ge(v_turned.sem, v_turned.at(base, *order[n - 1]))
                            dst, func = vT[:, :], ACT.Gelu_apprx_tanh if t[0] == "sv" else ACT.Copy
                        elif t[0] == "rg":
                            if t[1] > 0:
                                act.wait_ge(product.sem, product.at(base, "yr", t[1] - 1))
                            dst, func = ret_g, ACT.Silu
                        elif t[0] == "su":
                            dst, func = sg_u[t[1]], ACT.Gelu_apprx_tanh
                        else:
                            n = GATE_TILES.index(i)
                            dst, func = gates[n % 2], ACT.Sigmoid if t[0] == "gate" else ACT.Silu
                            if n >= 2:
                                u = TILES[GATE_TILES[n - 2]]
                                j = AT["proj" if u[0] == "gate" else "fup", u[1], u[2]]
                                act.wait_ge(stored_v.sem, stored_v.at(base, j))
                        act.activation(dst, src, func).then_inc(stored_s.sem, 1)
                    elif kind == "square":
                        n = SQ_KEYS.index(key)
                        if n >= 2:
                            act.wait_ge(stat_done.sem, stat_done.at(base, *SQ_KEYS[n - 2]))
                        if key[0] == "n":
                            src = xT[:, key[2], :]
                            if key[1] == 1:
                                act.wait_ge(stored_v.sem, stored_v.at(base, AT["wo", key[2]]))
                        elif key[0] == "c":
                            src = qk[key[2]]
                            act.wait_ge(stored_v.sem, stored_v.at(base, AT["q", key[1], 0] + key[2]))
                        else:
                            src = ret_y[:, :]
                            act.wait_ge(ret_copied.sem, ret_copied.at(base, key[1]))
                        act.activation(sq[:, n % 2, :], src, ACT.Square).then_inc(squared.sem, 1)
                    elif kind == "rstd":
                        n = STAT_GROUPS.index(key)
                        if n > 0:
                            act.wait_ge(rstd_ready.sem, rstd_ready.at(base, *STAT_GROUPS[n - 1]))
                        if key[0] == "n":
                            act.wait_ge(norm_summed.sem, norm_summed.at(base, *key))
                            src, cols, width = nsum[:, :], BLK, D_MODEL
                        else:
                            act.wait_ge(stat_done.sem, stat_done.at(base, *([k for k in keys("stat") if k[:2] == key][-1])))
                            cols, width = (24 if key[0] == "c" else BLK), P
                            src = stat_bank[:, 0:cols]
                        act.activation(std[:, 0:cols], src, ACT.Sqrt, bias=eps[:, 0:1], scale=1.0 / width).then_inc(
                            std_ready.sem, 1)
                    elif kind == "high":
                        if key[0] == "yc":
                            act.wait_ge(pv_done.sem, pv_done.at(base, key[1], BLK - 1))
                            src = out_bank[:, :]
                        else:
                            act.wait_ge(product.sem, product.at(base, *key))
                            src = prod[:, PROD_KEYS.index(key) % 2, :]
                        act.activation(parts(key)[0], src, ACT.Copy).then_inc(high_ready.sem, 1)
                    elif kind == "vtrans":
                        act.wait_ge(v_turned.sem, v_turned.at(base, *key))
                        src = turn_bank[T_USERS.index((kind,) + key) % 2][:, :].rearrange("p (b e) -> p b e", b=BLK)
                        if key[0] == "v":
                            dst = v_tok[key[2]]
                        elif key[0] == "rv":
                            dst = ret_v[:, :, :]
                        else:
                            dst = sg_v[:, :, key[1] * P:(key[1] + 1) * P]
                        act.activation(dst, src, ACT.Copy).then_inc(v_stored.sem, 1)
                    elif kind == "softmax":
                        h, b = key
                        act.wait_ge(max_ready.sem, max_ready.at(base, h, b))
                        at = SOFF[b] * P
                        for g, _, n in score_chunks(b):
                            e = act.activation(probs[:, at:at + n * P], probs[:, at:at + n * P], ACT.Exp,
                                               bias=negm[:, b:b + 1], scale=crow[:, g, b:b + 1],
                                               accum_out=den[:, b, g:g + 1])
                            at += n * P
                        e.then_inc(exp_ready.sem, 1)
                    elif kind == "ptrans":
                        h, b = key
                        if b > 0:
                            act.wait_ge(pv_done.sem, pv_done.at(base, h, b - 1))
                        for c, (first, n) in enumerate(trans_chunks(b)):
                            act.wait_ge(probs_turned.sem, probs_turned.at(base, h, b, c))
                            src = turn_bank[T_USERS.index(("ptrans", h, b, c)) % 2][:, 0:n * P]
                            act.activation(probsT[:, first * P:(first + n) * P], src, ACT.Copy).then_inc(
                                probsT_stored.sem, 1)
                    elif kind == "ocopy":
                        h, = key
                        act.wait_ge(ret_done.sem, ret_done.at(base, h))
                        if h > 0:
                            act.wait_ge(product.sem, product.at(base, "yr", h - 1))
                        act.activation(ret_y[:, :], out_bank[:, :], ACT.Copy).then_inc(ret_copied.sem, 1)
                    elif kind == "ln":
                        act.wait_ge(ln_var.sem, ln_var.at(base))
                        act.activation(lnstd[:, :], mv[:, :, 1], ACT.Sqrt, bias=eps[:, 0:1]).then_inc(ln_std.sem, 1)
                close(act, base, [part_high_w, stored_s, squared, std_ready, high_ready, v_stored, exp_ready,
                                  probsT_stored, ret_copied, ln_std])

        @block.vector
        def _(dve):
            dve.memset(ones[:, :], 1.0).then_inc(consts_set, 1)
            dve.memset(eps[:, :], EPS).then_inc(consts_set, 1)
            dve.wait_ge(const_loaded, PRE_CONST)
            dve.wait_ge(consts_set, 2)
            dve.sem_inc(layer_input, 1)
            with dve.Fori(0, DEPTH * STRIDE, STRIDE) as base:
                dve.get_value_cache().nocache = True
                chained = [0]

                def chain(ins):
                    ins.then_inc(vector_chain, 1)
                    chained[0] += 1
                    dve.wait_ge(vector_chain, base + chained[0])

                def product_slot(key):
                    n = PROD_KEYS.index(key)
                    if n >= 2:
                        dve.wait_ge(low_ready.sem, low_ready.at(base, *PROD_KEYS[n - 2]))
                    return prod[:, n % 2, :]

                tmp_read = []

                def tmp_free():
                    if tmp_read:
                        sig, key = tmp_read[-1]
                        dve.wait_ge(sig.sem, sig.at(base, *key))

                dve.wait_ge(vec_loaded, base + 16)
                chain(dve.tensor_tensor(gqk[:, :], vec[:, 20:21], vec[:, 21:22], ALU.mult))
                for kind, *key in STEPS:
                    key = tuple(key)
                    if kind == "split":
                        s, = key
                        dve.wait_ge(part_high_w.sem, part_high_w.at(base, s))
                        dve.tensor_tensor(w_low[:, s % PART_SLOTS, :, :], raw[:, s % RAW_SLOTS, :, :],
                                          w_high[:, s % PART_SLOTS, :, :], ALU.subtract).then_inc(part_low_w.sem, 1)
                    elif kind == "evac":
                        i, = key
                        t = TILES[i]
                        if t[0] in EVAC_BY_SCALAR:
                            continue
                        dve.wait_ge(tile_done.sem, tile_done.at(base, i))
                        src = main_bank[i % 2][:, :]
                        if t[0] in ("q", "k"):
                            dve.tensor_copy(qk[t[2] + (3 if t[0] == "k" else 0)], src).then_inc(stored_v.sem, 1)
                        elif t[0] in ("rq", "rk"):
                            dst = ret_q if t[0] == "rq" else ret_k
                            half = P // 2
                            tmp_free()
                            dve.tensor_tensor(dst, src, rot[:, 0, :], ALU.mult)
                            dve.tensor_tensor(tmp[0:half, :], main_bank[i % 2][half:P, :], rot[half:P, 1, :], ALU.mult)
                            chain(dve.tensor_tensor(tmp[half:P, :], main_bank[i % 2][0:half, :], rot[0:half, 1, :], ALU.mult))
                            dve.tensor_tensor(dst, dst, tmp[:, :], ALU.add).then_inc(stored_v.sem, 1)
                            tmp_read.append((stored_v, (i,)))
                        elif t[0] == "proj":
                            _, br, n = t
                            dve.wait_ge(stored_s.sem, stored_s.at(base, AT["gate", br, n]))
                            g = gates[GATE_TILES.index(AT["gate", br, n]) % 2]
                            if br == 2:
                                dve.tensor_tensor(merged[n], src, g, ALU.mult).then_inc(stored_v.sem, 1)
                            else:
                                tmp_free()
                                chain(dve.tensor_tensor(tmp[:, :], src, g, ALU.mult))
                                tmp_read.append((stored_v, (i,)))
                                if br == 0:
                                    dve.tensor_tensor(merged[n], merged[n], tmp[:, :], ALU.add).then_inc(stored_v.sem, 1)
                                else:
                                    dst = product_slot(("m", n))
                                    chain(dve.tensor_tensor(dst, merged[n], tmp[:, :], ALU.add))
                                    dve.sem_inc(product.sem, 1)
                                    dve.sem_inc(stored_v.sem, 1)
                        elif t[0] in ("wo", "down"):
                            dve.tensor_tensor(xT[:, t[-1], :], src, xT[:, t[-1], :], ALU.add).then_inc(stored_v.sem, 1)
                        else:
                            g = AT["fgate", t[1], t[2]]
                            dve.wait_ge(stored_s.sem, stored_s.at(base, g))
                            dst = product_slot(("f", t[1], t[2]))
                            chain(dve.tensor_tensor(dst, src, gates[GATE_TILES.index(g) % 2], ALU.mult))
                            dve.sem_inc(product.sem, 1)
                            dve.sem_inc(stored_v.sem, 1)
                    elif kind == "low":
                        dve.wait_ge(high_ready.sem, high_ready.at(base, *key))
                        hi, lo = parts(key)
                        src = out_bank[:, :] if key[0] == "yc" else prod[:, PROD_KEYS.index(key) % 2, :]
                        dve.tensor_tensor(lo, src, hi, ALU.subtract).then_inc(low_ready.sem, 1)
                    elif kind == "rstd":
                        cols = 24 if key[0] == "c" else BLK
                        if key[0] == "n":
                            dve.wait_ge(stat_done.sem, stat_done.at(base, "n", key[1], KT - 1))
                            dve.tensor_reduce(nsum[:, :], stat_bank[:, 0:4 * KT].rearrange("p (n b) -> p b n", b=BLK),
                                              AX_X, ALU.add).then_inc(norm_summed.sem, 1)
                        dve.wait_ge(std_ready.sem, std_ready.at(base, *key))
                        dve.reciprocal(rs[:, 0:cols], std[:, 0:cols]).then_inc(rstd_ready.sem, 1)
                        if key[0] == "c":
                            if key[1] > 0:
                                dve.wait_ge(exp_ready.sem, exp_ready.at(base, key[1] - 1, BLK - 1))
                            dve.wait_ge(rstd_ready.sem, rstd_ready.at(base, *key))
                            chain(dve.tensor_scalar(crow[:, :, :].rearrange("p g b -> p (g b)"), rs[:, 0:12], SCALE, None,
                                                    ALU.mult))
                    elif kind == "bcast":
                        order = keys("bcast")
                        n = order.index(key)
                        if n > 0:
                            dve.wait_ge(bcast_done.sem, bcast_done.at(base, *order[n - 1]))
                        group = ("c", key[1]) if key[0] == "k" else key
                        dve.wait_ge(rstd_ready.sem, rstd_ready.at(base, *group))
                        col = 12 + 4 * key[2] if key[0] == "k" else 0
                        dve.tensor_tensor(diag[:, :, :], ident[:, :].unsqueeze(1).broadcast_to([P, BLK, P]),
                                          rs[:, col:col + BLK].unsqueeze(2).broadcast_to([P, BLK, P]),
                                          ALU.mult).then_inc(diag_ready.sem, 1)
                    elif kind == "hprod":
                        w, n = key
                        dve.wait_ge(bcast_done.sem, bcast_done.at(base, "n", w))
                        dst = product_slot(("h", w, n))
                        dve.scalar_tensor_tensor(dst, xT[:, n, :], vec[:, 8 * w + n:8 * w + n + 1],
                                                 turn_bank[T_USERS.index(("bcast", "n", w)) % 2][:, :],
                                                 ALU.mult, ALU.mult).then_inc(product.sem, 1)
                    elif kind == "kscale":
                        h, g = key
                        dve.wait_ge(bcast_done.sem, bcast_done.at(base, "k", h, g))
                        dve.wait_ge(squared.sem, squared.at(base, "c", h, 3 + g))
                        dve.scalar_tensor_tensor(qk[3 + g], qk[3 + g], gqk[:, 0:1],
                                                 turn_bank[T_USERS.index(("bcast", "k", h, g)) % 2][:, :],
                                                 ALU.mult, ALU.mult).then_inc(k_scaled.sem, 1)
                    elif kind == "scores":
                        h, b = key
                        at, m = SOFF[b] * P, (1 if b == 0 else 0)
                        for c, (g, _, n) in enumerate(score_chunks(b)):
                            m = (2 - n) if g == 0 else 2 + 4 * (g - 1) + 4 - n
                            dve.wait_ge(scored.sem, scored.at(base, "scores", h, b, c))
                            own_wait(dve)
                            dve.tensor_tensor_reduce(probs[:, at:at + n * P],
                                                     score_bank[S_USERS.index(("scores", h, b, c)) % 2][:, 0:n * P],
                                                     mask[:, m:m + n, :].rearrange("p a n -> p (a n)"), 1.0, -3e38,
                                                     ALU.add, ALU.max, smax[:, b, g:g + 1]).then_inc(score_taken.sem, 1)
                            at += n * P
                        dve.wait_ge(score_taken.sem, score_taken.at(base, "scores", h, b, 2))
                        chain(dve.tensor_tensor(smax2[:, b, :], smax[:, b, :], crow[:, :, b], ALU.mult))
                        dve.tensor_reduce(negm[:, b:b + 1], smax2[:, b, :], AX_X, ALU.max, negate=True).then_inc(
                            max_ready.sem, 1)
                    elif kind == "softmax":
                        h, b = key
                        dve.wait_ge(exp_ready.sem, exp_ready.at(base, h, b))
                        chain(dve.tensor_reduce(dsum[:, b:b + 1], den[:, b, :], AX_X, ALU.add))
                        chain(dve.reciprocal(rden[:, b:b + 1], dsum[:, b:b + 1]))
                        p = probs[:, SOFF[b] * P:(SOFF[b] + SBLK[b]) * P]
                        dve.tensor_scalar(p, p, rden[:, b:b + 1], None, ALU.mult).then_inc(probs_ready.sem, 1)
                    elif kind == "rscore":
                        h, m = key
                        n = SEQ - m * P
                        dve.wait_ge(scored.sem, scored.at(base, "rscore", h, m))
                        dve.wait_ge(decay_loaded[h % 2], base + 16 * (h // 2 + 1))
                        dve.tensor_tensor(ret_s[:, RS_OFF[m]:RS_OFF[m] + n],
                                          score_bank[S_USERS.index(("rscore", h, m)) % 2][:, 0:n],
                                          decay_sb[:, h % 2, 0:n], ALU.mult).then_inc(score_taken.sem, 1)
                    elif kind == "rscale":
                        h, = key
                        dve.wait_ge(bcast_done.sem, bcast_done.at(base, "r", h))
                        dve.wait_ge(squared.sem, squared.at(base, "r", h))
                        dve.wait_ge(stored_s.sem, stored_s.at(base, AT["rg", h]))
                        dst = product_slot(("yr", h))
                        tmp_free()
                        tmp_read.append((product, ("yr", h)))
                        chain(dve.scalar_tensor_tensor(tmp[:, :], ret_y[:, :], vec[:, 16 + h:17 + h],
                                                       turn_bank[T_USERS.index(("bcast", "r", h)) % 2][:, :],
                                                       ALU.mult, ALU.mult))
                        dve.tensor_tensor(dst, tmp[:, :], ret_g, ALU.mult).then_inc(product.sem, 1)
                    elif kind == "ln":
                        dve.wait_ge(spatial_loaded, base + 32)
                        chain(dve.tensor_tensor(sgw[:, :, :], sgw[:, :, :],
                                                mask[:, 10:11, :].broadcast_to([P, HEADS, P]), ALU.mult))
                        for c in range(HEADS):
                            dve.wait_ge(v_stored.sem, v_stored.at(base, "sv", c))
                        for b in range(BLK):
                            last = dve.bn_stats(bn6[:, b, :], sg_v[:, b, :])
                        chain(last)
                        own_wait(dve)
                        for b in range(BLK):
                            last = dve.bn_aggr(mv[:, b, :], bn6[:, b, :])
                        last.then_inc(ln_var.sem, 1)
                        dve.wait_ge(ln_std.sem, ln_std.at(base))
                        chain(dve.reciprocal(lnrs[:, :], lnstd[:, :]))
                        for b in range(BLK):
                            last = dve.tensor_scalar(sg_v[:, b, :], sg_v[:, b, :], mv[:, b, 0:1], lnrs[:, b:b + 1],
                                                     ALU.subtract, ALU.mult)
                        chain(last)
                        chain(dve.tensor_tensor(sg_v, sg_v, row[:, 0:1, :].broadcast_to([P, BLK, SEQ]), ALU.mult))
                        dve.tensor_tensor(sg_v, sg_v, row[:, 1:2, :].broadcast_to([P, BLK, SEQ]), ALU.add).then_inc(
                            ln_done.sem, 1)
                    elif kind == "mix":
                        g, = key
                        dve.wait_ge(scored.sem, scored.at(base, "mix", g))
                        dve.wait_ge(stored_s.sem, stored_s.at(base, AT["su", g]))
                        dst = product_slot(("ys", g))
                        src = score_bank[S_USERS.index(("mix", g)) % 2][:, :].rearrange("p (b n) -> p b n", b=BLK)
                        tmp_free()
                        tmp_read.append((product, ("ys", g)))
                        ins = dve.tensor_tensor(tmp[:, :].rearrange("p (b n) -> p b n", b=BLK), src,
                                                row[:, 2:3, g * P:(g + 1) * P].broadcast_to([P, BLK, P]), ALU.add)
                        ins.then_inc(score_taken.sem, 1)
                        dve.wait_ge(score_taken.sem, score_taken.at(base, "mix", g))
                        dve.tensor_tensor(dst, tmp[:, :], sg_u[g], ALU.mult).then_inc(product.sem, 1)
                close(dve, base, [part_low_w, stored_v, norm_summed, rstd_ready, diag_ready, product, low_ready,
                                  k_scaled, score_taken, max_ready, probs_ready, ln_var, ln_done])
                dve.wait_ge(vector_chain, base + chained[0])
                dve.sem_inc(vector_chain, STRIDE - chained[0])
                dve.sem_inc(layer_input, STRIDE)



def _columns():
    ka, va, ga, ub, vb = 512, 1024, 1536, 2048, 2560
    qc = 3072
    kc, vc, gates = qc + 1536, qc + 3072, qc + 4608

    def of(t):
        if t[0] in "qkv":
            return {"q": qc, "k": kc, "v": vc}[t[0]] + t[2] * 512 + t[1] * P
        if t[0] == "gate":
            return gates + t[1] * D_MODEL + t[2] * P
        return {"rq": 0, "rk": ka, "rv": va, "rg": ga, "su": ub, "sv": vb}[t[0]] + t[1] * P
    return of


def _weights(w_in, w_branch, w_o, w_gate_up, w_down):
    of = _columns()
    out = np.empty((DEPTH * SLABS + RAW_SLOTS, P, 8, P), np.float32)
    for layer in range(DEPTH):
        for t, blocks in zip(TILES, BLOCKS):
            if t[0] == "proj":
                src, col, row0 = w_branch[layer, t[1]], t[2] * P, 0
            elif t[0] == "wo":
                src, col, row0 = w_o[layer], t[1] * P, 0
            elif t[0] in ("fgate", "fup"):
                src, col, row0 = w_gate_up[layer], (D_FF if t[0] == "fup" else 0) + (t[1] * FF_HALF + t[2]) * P, 0
            elif t[0] == "down":
                src, col, row0 = w_down[layer], t[2] * P, t[1] * FF_HALF * P
            else:
                src, col, row0 = w_in[layer], of(t), 0
            for s, place, k in blocks:
                r = row0 + k * P
                out[layer * SLABS + s, :, place, :] = src[r:r + P, col:col + P]
    out[DEPTH * SLABS:] = out[:RAW_SLOTS]
    return out.reshape(-1, P, 8 * P)


def _constants():
    f = np.float32
    half = P // 2
    inv = (f(1.0) / (f(ROPE_BASE) ** (np.arange(half, dtype=f) / f(half)))).astype(f)
    ang = (np.arange(SEQ, dtype=f)[:, None] * inv[None, :]).astype(f)
    cos, sin = np.cos(ang).T.astype(f), np.sin(ang).T.astype(f)
    rotation = np.stack([np.concatenate([cos, cos]), np.concatenate([sin, -sin])], axis=1)
    log_g = np.log1p(-(2.0 ** (-5.0 - np.arange(HEADS))))
    dist = np.arange(SEQ)[None, :] - np.arange(P)[:, None]
    decay = np.where(dist[None] >= 0, np.exp(log_g[:, None, None] * np.maximum(dist, 0)) * SCALE, 0.0).astype(f)
    q, k = np.arange(P)[:, None], np.arange(P)[None, :]
    causal = k <= q
    blocks = [(q + P - k) <= DILATIONS[0][0], causal]
    for _, d in DILATIONS[1:]:
        same = (q - k) % d == 0
        blocks += [same] * 3 + [same & causal]
    masks = [np.where(b, 0.0, NEG) for b in blocks] + [np.where(q <= k, 1.0, 0.0)]
    masks = (np.stack(masks, axis=1).astype(f).view(np.uint32) >> 16).astype(np.uint16)
    return rotation.astype(f), decay, masks, np.eye(P, dtype=f)


def kernel(x, g_mix, w_in, ret_norm_g, sg_ln_g, sg_ln_b, sg_w, sg_b, dil_q_norm_g, dil_k_norm_g, w_branch, w_o,
           g_ffn, w_gate_up, w_down):
    import concourse.bacc as bacc
    from concourse.bass_utils import run_bass_kernel_spmd

    def per_layer(a, n):
        return np.asarray(a).reshape(DEPTH, n, P).transpose(0, 2, 1)

    def and_again(a):
        return np.ascontiguousarray(np.concatenate([a, a[-1:]]))

    rotation, decay, masks, ident = _constants()
    arrays = {
        "x_t": np.ascontiguousarray(np.asarray(x)[0].T.reshape(KT, P, SEQ).transpose(1, 0, 2)),
        "weights": _weights(*(np.asarray(a) for a in (w_in, w_branch, w_o, w_gate_up, w_down))),
        "vecs": and_again(np.concatenate([per_layer(g_mix, KT), per_layer(g_ffn, KT), per_layer(ret_norm_g, HEADS),
                                          per_layer(dil_q_norm_g, 1), per_layer(dil_k_norm_g, 1)], axis=2)),
        "spatial": and_again(np.asarray(sg_w).transpose(0, 3, 1, 2)),
        "rows": and_again(np.stack([np.asarray(sg_ln_g), np.asarray(sg_ln_b), np.asarray(sg_b).reshape(DEPTH, -1)],
                                   axis=1)),
        "rotation": rotation, "decay": decay, "masks": masks, "ident": ident,
    }
    nc = bacc.Bacc("TRN2", target_bir_lowering=False, num_devices=1)
    aps = [nc.dram_tensor(name, a.shape, mybir.dt.from_np(a.dtype), kind="ExternalInput").ap()
           for name, a in arrays.items()]
    out = nc.dram_tensor("out_t", (P, KT, SEQ), F32, kind="ExternalOutput").ap()
    build(nc, *aps, out)
    r = run_bass_kernel_spmd(nc, [arrays], core_ids=[0])
    y = r.results[0]["out_t"]
    return np.ascontiguousarray(y.transpose(2, 1, 0).reshape(1, SEQ, D_MODEL))
```

```python
from contextlib import ExitStack

import numpy as np

import concourse.bass as bass
from concourse import mybir

P = 128
D_MODEL = 1024
SEQ = 512
DEPTH = 2
EPS = 1e-6
HEADS = 4
N_GROUP = 3
D_FF = 2816
KT = D_MODEL // P
BLK = SEQ // P
FF_HALF = D_FF // P // 2
DILATIONS = ((128, 1), (512, 4), (2048, 16))
ROPE_BASE = 10000.0
NEG = -1e30
SCALE = float(P) ** -0.5

RAW_SLOTS = 3
PART_SLOTS = 3

ALU = mybir.AluOpType
ACT = mybir.ActivationFunctionType
AX_X = mybir.AxisListType.X
F32 = mybir.dt.float32
F32R = mybir.dt.float32r
BF16 = mybir.dt.bfloat16



def tiles_of_layer():
    t = []
    for h in range(HEADS):
        t += [("k", h, g) for g in range(N_GROUP)] + [("q", h, g) for g in range(N_GROUP)]
        t += [("v", h, g) for g in range(N_GROUP)]
    for h in range(HEADS):
        t += [("rq", h), ("rk", h), ("rv", h), ("rg", h)]

    def gated(branch):
        out = []
        for n in range(0, KT, 2):
            out += [("gate", branch, n), ("gate", branch, n + 1), ("proj", branch, n), ("proj", branch, n + 1)]
        return out

    t += gated(2)
    t += [("sv", c) for c in range(HEADS)] + [("su", c) for c in range(HEADS)]
    t += gated(0) + gated(1)
    t += [("wo", n) for n in range(KT)]
    for half in range(2):
        for j in range(FF_HALF):
            t += [("fgate", half, j), ("fup", half, j)]
        t += [("down", half, n) for n in range(KT)]
    return t


TILES = tiles_of_layer()
AT = {t: i for i, t in enumerate(TILES)}


def blocks_of_tiles():
    out, n = [], 0
    for t in TILES:
        k = 4 if t[0] == "proj" else FF_HALF if t[0] == "down" else KT
        out.append([((n + i) // 8, (n + i) % 8, i) for i in range(k)])
        n += k
    assert n % 8 == 0
    return out, n // 8


BLOCKS, SLABS = blocks_of_tiles()
STRIDE = 16 * SLABS
FIRST_USE = {s: min(i for i, b in enumerate(BLOCKS) if any(x[0] == s for x in b)) for s in range(SLABS)}
LAST_BLOCK = {b[0]: (i, b) for i, bs in enumerate(BLOCKS) for b in bs}
PART_SLOT = [s % PART_SLOTS for s in range(SLABS - PART_SLOTS)] + list(range(PART_SLOTS))
SLOT_BEFORE = [next((u for u in range(s - 1, -1, -1) if PART_SLOT[u] == PART_SLOT[s]), SLABS - PART_SLOTS + s)
               for s in range(SLABS)]
SPLIT_AHEAD = 2

PROJECTION_EVENTS = []
for _i, _bs in enumerate(BLOCKS):
    PROJECTION_EVENTS += [("slab", b[0]) for b in _bs[:-1] if LAST_BLOCK[b[0]] == (_i, b)] + [(_i,)]

EVAC_BY_SCALAR = {"v", "rv", "sv", "rg", "su", "gate", "fgate"}


def score_chunks(b):
    return [(0, max(b - 1, 0), min(b, 1) + 1), (1, 0, b + 1), (2, 0, b + 1)]


SBLK = [sum(c[2] for c in score_chunks(b)) for b in range(BLK)]
SOFF = [sum(SBLK[:b]) for b in range(BLK)]


def trans_chunks(b):
    return [(i, min(4, SBLK[b] - i)) for i in range(0, SBLK[b], 4)]


def schedule():
    pre = {i: [] for i in range(len(TILES))}
    post = {i: [] for i in range(len(TILES))}
    for h in range(HEADS):
        t = AT["k", h, 0]
        for j in range(N_GROUP):
            for first, name in ((t, "ck"), (t + N_GROUP, "cq")):
                post[first + j] += [("square", name, h, j)]
                pre[first + j + 1] += [("stat", name, h, j)]
        pre[t + 3] += [("rstd", "ck", h)]
        pre[t + 6] += [("rstd", "cq", h)]
        for g in range(N_GROUP):
            pre[t + 4 + g] += [("bcast", "k", h, g), ("kscale", h, g)]
            pre[t + 7 + g] += [("vtrans", "v", h, g)]
        pre[t + 7] += [("scores", h, 0), ("scores", h, 1), ("softmax", h, 0)]
        pre[t + 8] += [("scores", h, 2), ("softmax", h, 1)]
        pre[t + 9] += [("scores", h, 3), ("softmax", h, 2), ("ptrans", h, 0), ("softmax", h, 3)]
        for b in range(BLK):
            pre[t + 10 + b] += [("pv", h, b)]
            if b < BLK - 1:
                pre[t + 10 + b] += [("ptrans", h, b + 1)]
        pre[t + 13] += [("high", "yc", h), ("low", "yc", h)]
    for h in range(HEADS):
        t = AT["rq", h]
        pre[t + 2] += [("rscore", h, m) for m in range(2)]
        pre[t + 3] += [("vtrans", "rv", h)] + [("rscore", h, m) for m in range(2, BLK)]
        pre[t + 5] += [("rpv", h), ("ocopy", h), ("square", "r", h)]
        pre[t + 6] += [("stat", "r", h), ("rstd", "r", h)]
        pre[t + 8] += [("bcast", "r", h), ("rscale", h), ("high", "yr", h), ("low", "yr", h)]
    t = AT["sv", 0]
    for c in range(HEADS):
        pre[t + c + 1] += [("vtrans", "sv", c)]
    for b in range(BLK):
        pre[t + 5 + b] += [("ln", b)]
    for g in range(HEADS):
        pre[t + 10 + g] += [("mix", g), ("high", "ys", g), ("low", "ys", g)]
    for n in range(KT):
        post[AT["proj", 1, n]] += [("high", "m", n), ("low", "m", n)]
        for tile, which in ((AT["wo", n], 1), (AT["down", 1, n], "next")):
            post[tile] += [("square", "n", which, n)]
            if n < KT - 1:
                pre[tile + 1] += [("stat", "n", which, n)]
            else:
                pre[tile] += [("load_sqrt",)]
                post[tile] += [("stat", "n", which, n)]
    for half in range(2):
        for j in range(FF_HALF):
            post[AT["fup", half, j]] += [("high", "f", half, j), ("low", "f", half, j)]

    def norm(w):
        out = [("rstd", "n", w), ("bcast", "n", w), ("hprod", w, 0), ("high", "h", w, 0)]
        for n in range(1, KT):
            out += [("hprod", w, n), ("high", "h", w, n), ("low", "h", w, n - 1)]
            if w == 0 and n == 3:
                out += [("split", s) for s in range(SPLIT_AHEAD, PART_SLOTS)]
        return out + [("low", "h", w, KT - 1)]

    post[AT["wo", KT - 1]] += norm(1)
    pre[AT["down", 1, KT - 2]] += [("fill_split",), ("split", "next", 0)]
    pre[AT["down", 1, KT - 1]] += [("split", "next", 1)]
    pre[AT["down", 1, 0]] = [("fill_ahead",)] + pre[AT["down", 1, 0]]

    steps = norm(0)
    split = PART_SLOTS
    for i in range(len(TILES)):
        if i in AFTER_NORM:
            steps.append(("main", i, i + 1))
        elif i - 1 not in AFTER_NORM:
            steps.append(("main", i))
        while split < SLABS and FIRST_USE[split - PART_SLOTS + 1] <= i + 1 and LAST_BLOCK[SLOT_BEFORE[split]][0] <= i:
            steps.append(("split", split))
            split += 1
        steps += pre[i] + [("evac", i)] + post[i]
    assert split == SLABS
    return steps


AFTER_NORM = (AT["k", 0, 0], AT["fgate", 0, 0])
STEPS = schedule()


def keys(kind, *starts):
    return [s[1:] for s in STEPS if s[0] == kind and (not starts or s[1] in starts)]


def chunk_keys(kind, chunks):
    return [k + (c,) for k in keys(kind) for c in range(len(chunks(k[1])))]


class Signal:

    def __init__(self, sem, events, ahead=()):
        self.sem = sem
        events = [k for k in events if "next" not in k]
        self.number = {k: i + 1 for i, k in enumerate(list(ahead) + events)}
        self.count = len(events)
        self.ahead = len(ahead)
        assert len(self.number) == len(events) + len(ahead) < STRIDE

    def at(self, base, *key):
        if "next" in key:
            key = tuple(k for k in key if k != "next")
            return base + STRIDE + (self.number[key] if key in self.number else self.number[("n", 0) + key[1:]])
        return base + self.number[key]


T_USERS = []
for _s in STEPS:
    if _s[0] in ("bcast", "vtrans"):
        T_USERS.append(_s)
    elif _s[0] == "ptrans":
        T_USERS += [_s + (c,) for c in range(len(trans_chunks(_s[2])))]
S_USERS = []
for _s in STEPS:
    if _s[0] == "scores":
        S_USERS += [_s + (c,) for c in range(3)]
    elif _s[0] in ("rscore", "mix"):
        S_USERS.append(_s)
SQ_KEYS = keys("square")
MAIN_TILES = [(i,) for i in range(len(TILES))]
NORM_AHEAD = [("n", 0, n) for n in range(KT)]
STAT_GROUPS = keys("rstd")
PROD_KEYS = [s[1:] for s in STEPS if s[0] == "high" and s[1] != "yc"]
GATE_TILES = [i for i, t in enumerate(TILES) if t[0] in ("gate", "fgate")]


def build(nc, x_in, weights, vecs, spatial, rows, rotation, decay, masks, ident_in, out):
    with ExitStack() as ctx:
        def sb(name, shape, dt=F32):
            return ctx.enter_context(nc.sbuf_tensor(name, shape, dt))

        def signal(name, events, ahead=()):
            return Signal(ctx.enter_context(nc.semaphore(name)), events, ahead)

        raw = sb("raw", [P, RAW_SLOTS, 8, P])
        w_high = sb("w_high", [P, PART_SLOTS, 8, P], F32R)
        w_low = sb("w_low", [P, PART_SLOTS, 8, P], F32R)
        xT = sb("xT", [P, KT, SEQ])
        h_high = sb("h_high", [P, KT, SEQ], F32R)
        h_low = sb("h_low", [P, KT, SEQ], F32R)
        in_high = sb("in_high", [P, 12, SEQ], F32R)
        in_low = sb("in_low", [P, 12, SEQ], F32R)
        work = sb("work", [P, 19, SEQ])
        ret_v = sb("ret_v", [P, BLK, P])
        tmp = sb("tmp", [P, SEQ])
        prod = sb("prod", [P, 2, SEQ])
        sq = sb("sq", [P, 2, SEQ])
        vT = sb("vT", [P, SEQ])
        decay_sb = sb("decay_sb", [P, 2, SEQ])
        rot = sb("rot", [P, 2, SEQ])
        mask_bits = sb("mask_bits", [P, 11, P], mybir.dt.uint16)
        mask = mask_bits[:, :, :].bitcast(BF16)
        ident = sb("identity", [P, P])
        ones = sb("ones", [P, P])
        vec = sb("vec", [P, 22])
        sgw = sb("sgw", [P, HEADS, P])
        row = sb("row", [P, 3, SEQ])
        eps = sb("eps", [P, 1])
        eps_q = sb("eps_q", [P, 1])
        sqrt_out = sb("sqrt_out", [P, 1])
        gqk = sb("gqk", [P, 1])
        nsum = sb("nsum", [P, BLK])
        std = sb("std", [P, N_GROUP * BLK])
        rs = sb("rs", [P, N_GROUP * BLK])
        crow = sb("crow", [P, N_GROUP, BLK])
        smax = sb("smax", [P, BLK, N_GROUP])
        smax2 = sb("smax2", [P, BLK, N_GROUP])
        negm = sb("negm", [P, BLK])
        den = sb("den", [P, BLK, N_GROUP])
        dsum = sb("dsum", [P, BLK])
        rden = sb("rden", [P, BLK])
        bn6 = sb("bn6", [P, BLK, 6])
        mv = sb("mv", [P, BLK, 2])
        lnstd = sb("lnstd", [P, BLK])
        lnrs = sb("lnrs", [P, BLK])

        qk = [work[:, j, :] for j in range(6)]
        v_tok = [work[:, 6 + g, :].rearrange("p (b e) -> p b e", b=BLK) for g in range(N_GROUP)]
        probs = work[:, 9:16, :].rearrange("p a n -> p (a n)")
        probsT = work[:, 16:19, :].rearrange("p a n -> p (a n)")
        ret_s = work[:, 0:3, :].rearrange("p a n -> p (a n)")
        ret_q, ret_k, ret_y = work[:, 3, :], work[:, 4, :], work[:, 8, :]
        ret_g = [work[:, 5 + i, :] for i in range(2)]
        merged = [work[:, 9 + n, :] for n in range(KT)]
        gates = [work[:, 17 + n, :] for n in range(2)]
        sg_u = [work[:, n, :] for n in range(HEADS)]
        sg_v = work[:, 4:8, :]
        RS_OFF = [m * SEQ - P * m * (m - 1) // 2 for m in range(BLK)]

        psum = [ctx.enter_context(nc.psum_tensor(f"bank{i}", [P, SEQ], F32)) for i in range(8)]
        main_bank, score_bank, turn_bank = psum[0:2], psum[2:4], psum[4:6]
        out_bank, stat_bank = psum[6], psum[7]

        raw_loaded = [signal(f"raw_loaded{r}", [(s, i) for s in range(r, SLABS, RAW_SLOTS) for i in range(16)])
                      for r in range(RAW_SLOTS)]
        split_ahead = [(s,) for s in range(SPLIT_AHEAD)]
        part_high_w = signal("weight_high_ready", keys("split"), split_ahead)
        part_low_w = signal("weight_low_ready", keys("split"), split_ahead)
        tile_done = signal("slab_used_tile_done", PROJECTION_EVENTS)
        slab_used = Signal(tile_done.sem, PROJECTION_EVENTS)
        for i, bs in enumerate(BLOCKS):
            for s in {b[0] for b in bs}:
                if LAST_BLOCK[s] == (i, bs[-1]):
                    slab_used.number["slab", s] = tile_done.number[i,]
        stored_v = signal("tile_stored_by_vector", [k for k in keys("evac") if TILES[k[0]][0] not in EVAC_BY_SCALAR])
        stored_s = signal("tile_stored_by_scalar", [k for k in keys("evac") if TILES[k[0]][0] in EVAC_BY_SCALAR])
        squared = signal("squared", keys("square"), NORM_AHEAD)
        stat_done = signal("stat_done", keys("stat"), NORM_AHEAD)
        norm_summed = signal("norm_summed", keys("rstd", "n"))
        std_ready = signal("std_ready", keys("rstd"))
        rstd_ready = signal("rstd_ready", keys("rstd"))
        bcast_done = signal("bcast_done", keys("bcast"))
        product = signal("product_ready", PROD_KEYS)
        high_ready = signal("high_ready", keys("high"))
        low_ready = signal("low_ready", keys("low"))
        k_scaled = signal("k_scaled", keys("kscale"))
        v_turned = signal("v_turned", keys("vtrans"))
        v_stored = signal("v_stored", keys("vtrans"))
        scored = signal("scored", [u for u in S_USERS])
        score_taken = signal("score_taken", [u for u in S_USERS])
        max_ready = signal("max_ready", keys("scores"))
        exp_ready = signal("exp_ready", keys("softmax"))
        probs_ready = signal("probs_ready", keys("softmax"))
        probs_turned = signal("probs_turned", chunk_keys("ptrans", trans_chunks))
        probsT_stored = signal("probsT_stored", chunk_keys("ptrans", trans_chunks))
        pv_done = signal("pv_done", keys("pv"))
        ret_done = signal("ret_done", keys("rpv"))
        ret_copied = signal("ret_copied", keys("ocopy"))
        ln_var = signal("ln_var_ready", [()])
        ln_std = signal("ln_std_ready", [()])
        sqrt_loaded = signal("sqrt_loaded", [(i,) for i in range(len(keys("load_sqrt")))])
        ln_done = signal("ln_done", keys("ln"))
        vector_chain = ctx.enter_context(nc.semaphore("vector_chain"))
        layer_input = ctx.enter_context(nc.semaphore("layer_input"))
        const_loaded = ctx.enter_context(nc.semaphore("const_loaded"))
        consts_set = ctx.enter_context(nc.semaphore("consts_set"))
        vec_loaded = ctx.enter_context(nc.semaphore("vec_loaded"))
        spatial_loaded = ctx.enter_context(nc.semaphore("spatial_loaded"))
        decay_loaded = [ctx.enter_context(nc.semaphore(f"decay_loaded{i}")) for i in range(2)]
        wait_carried = ctx.enter_context(nc.semaphore("wait_carried"))
        out_stored = ctx.enter_context(nc.semaphore("out_stored"))
        x_loaded = [ctx.enter_context(nc.semaphore(f"x_loaded{n}")) for n in range(KT)]
        PRE_CONST = 16 * 3

        def layer_base(eng, layer):
            base = eng.snap(layer * STRIDE)
            eng.get_value_cache().nocache = True
            return base

        def own_wait(eng):
            eng.sem_inc(wait_carried, 1)

        def sq_slot(key):
            return (key[2] if key[:2] == ("n", 0) else SQ_KEYS.index(key)) % 2

        def rstd_of(key):
            return ("ck", key[1]) if key[0] == "k" else key

        def tile_stored(i):
            return stored_s if TILES[i][0] in EVAC_BY_SCALAR else stored_v

        def wait_tile_stored(eng, base, i):
            eng.wait_ge(tile_stored(i).sem, tile_stored(i).at(base, i))

        def wait_turn_bank(pe, base, n):
            if n < 2:
                return
            u = T_USERS[n - 2]
            if u[0] == "vtrans":
                pe.wait_ge(v_stored.sem, v_stored.at(base, *u[1:]))
            elif u[0] == "ptrans":
                pe.wait_ge(probsT_stored.sem, probsT_stored.at(base, *u[1:]))
            elif u[1] == "n":
                pe.wait_ge(product.sem, product.at(base, "h", u[2], KT - 1))
            elif u[1] == "k":
                pe.wait_ge(k_scaled.sem, k_scaled.at(base, *u[2:]))
            else:
                pe.wait_ge(product.sem, product.at(base, "yr", u[2]))

        def fill_up(eng, sig):
            eng.sem_inc(sig.sem, STRIDE - sig.ahead - sig.count)

        def close(eng, base, sigs):
            for sig in sigs:
                eng.wait_ge(sig.sem, base + sig.ahead + sig.count)
                fill_up(eng, sig)

        def parts(key):
            kind = key[0]
            if kind == "h":
                return h_high[:, key[2], :], h_low[:, key[2], :]
            n = {"yc": 0, "ys": 0, "yr": 4, "m": 4, "f": 0}[kind] + key[-1]
            return in_high[:, n, :], in_low[:, n, :]

        def input_tile(i, k):
            t = TILES[i]
            key = {"proj": lambda: ({2: "yc", 0: "yr", 1: "ys"}[t[1]], k),
                   "wo": lambda: ("m", k), "down": lambda: ("f", t[1], k)}.get(
                t[0], lambda: ("h", 1 if t[0] in ("fgate", "fup") else 0, k))()
            return key, parts(key)

        block = ctx.enter_context(nc.Block())

        @block.sync
        def _(sp):
            for n in range(KT):
                sp.dma_start(xT[:, n, :], x_in[:, n, :]).then_inc(x_loaded[n], 16)

            def load(base, s, row_of):
                slot = s % RAW_SLOTS
                sp.dma_start(raw[:, slot, :, :].rearrange("p a n -> p (a n)"),
                             weights[bass.ds(row_of, 1)].rearrange("a p n -> (a p) n")).then_inc(
                    raw_loaded[slot].sem, 16)

            def load_vecs(layer):
                sp.dma_start(vec[:, :], vecs[bass.ds(layer, 1)].rearrange("a p n -> (a p) n")).then_inc(
                    vec_loaded, 16)

            def load_spatial(layer):
                sp.dma_start(sgw[:, :, :], spatial[bass.ds(layer, 1)].rearrange("a p g n -> (a p) g n")).then_inc(
                    spatial_loaded, 16)
                sp.dma_start(row[:, :, :].rearrange("p r n -> p (r n)"),
                             rows[bass.ds(layer, 1)].rearrange("a r n -> (a r n)").partition_broadcast(P)).then_inc(
                    spatial_loaded, 16)

            def load_decay(base, h):
                if h >= 2:
                    sp.wait_ge(score_taken.sem, score_taken.at(base, "rscore", h - 2, BLK - 1))
                sp.dma_start(decay_sb[:, h % 2, :], decay[h]).then_inc(decay_loaded[h % 2], 16)

            def behind(tile):
                return max(b[0] for b in BLOCKS[AT[tile]]) + RAW_SLOTS

            decay_at = {behind(("k", 1, h)): h for h in range(2)} | {behind(("rg", h - 1)): h for h in range(2, HEADS)}

            for s in range(RAW_SLOTS):
                load(0, s, s)
            load_vecs(0)
            load_spatial(0)
            sp.dma_start(rot[:, :, :], rotation).then_inc(const_loaded, 16)
            sp.dma_start(mask_bits[:, :, :], masks).then_inc(const_loaded, 16)
            sp.dma_start(ident[:, :], ident_in).then_inc(const_loaded, 16)
            with sp.Fori(0, DEPTH) as layer:
                base = layer_base(sp, layer)
                for s in range(RAW_SLOTS, SLABS + RAW_SLOTS):
                    slot = (s if s < SLABS else s - SLABS) % RAW_SLOTS
                    before = s - RAW_SLOTS if s < SLABS else max(u for u in range(SLABS) if u % RAW_SLOTS == slot)
                    sp.wait_ge(part_low_w.sem, part_low_w.at(base, before))
                    if s >= SLABS:
                        fill_up(sp, raw_loaded[slot])
                    load(base, slot if s >= SLABS else s, layer * SLABS + s)
                    if s in decay_at:
                        load_decay(base, decay_at[s])
                    if s == behind(("proj", 1, 0)):
                        sp.wait_ge(score_taken.sem, score_taken.at(base, "mix", HEADS - 1))
                        sp.wait_ge(spatial_loaded, base + 32)
                        sp.sem_inc(spatial_loaded, STRIDE - 32)
                        load_spatial(layer + 1)
                    if s == behind(("fgate", 0, 4)):
                        sp.wait_ge(product.sem, product.at(base, "h", 1, KT - 1))
                        sp.wait_ge(vec_loaded, base + 16)
                        sp.sem_inc(vec_loaded, STRIDE - 16)
                        load_vecs(layer + 1)
                for i in range(2):
                    sp.wait_ge(decay_loaded[i], base + 32)
                    sp.sem_inc(decay_loaded[i], STRIDE - 32)
            for s in range(RAW_SLOTS):
                sp.wait_ge(raw_loaded[s].sem, DEPTH * STRIDE + 16)
            sp.wait_ge(vec_loaded, DEPTH * STRIDE + 16)
            sp.wait_ge(spatial_loaded, DEPTH * STRIDE + 32)
            sp.wait_ge(layer_input, DEPTH * STRIDE + 1)
            sp.dma_start(out, xT[:, :, :]).then_inc(out_stored, 16)
            sp.wait_ge(out_stored, 16)

        @block.tensor
        def _(pe):
            pe.wait_ge(const_loaded, PRE_CONST)
            pe.wait_ge(consts_set, 3)

            def matmul(o, w, m, start, stop):
                return pe.matmul(o, w, m, start=start, stop=stop)

            seen_inputs = set()

            def main(base, *tiles):
                for i in tiles:
                    if i >= 2:
                        wait_tile_stored(pe, base, i - 2)
                for n in range(len(BLOCKS[tiles[0]])):
                    for i in tiles:
                        o, blocks = main_bank[i % 2], BLOCKS[i]
                        s, place, k = blocks[n]
                        if FIRST_USE[s] == i and (n == 0 or blocks[n - 1][0] != s):
                            pe.wait_ge(part_low_w.sem, part_low_w.at(base, s))
                        key, (hi, lo) = input_tile(i, k)
                        if key not in seen_inputs:
                            seen_inputs.add(key)
                            pe.wait_ge(low_ready.sem, low_ready.at(base, *key))
                        wh, wl = w_high[:, PART_SLOT[s], place, :], w_low[:, PART_SLOT[s], place, :]
                        matmul(o[:, :], wh, hi, n == 0, False)
                        matmul(o[:, :], wh, lo, False, False)
                        last = matmul(o[:, :], wl, hi, False, n == len(blocks) - 1)
                        if n == len(blocks) - 1:
                            last.then_inc(tile_done.sem, 1)
                        elif LAST_BLOCK[s] == (i, (s, place, k)):
                            last.then_inc(slab_used.sem, 1)

            def stat(base, key):
                group = key[:2]
                if key[2:] in ((), (0,)) and group != ("n", 0):
                    n = STAT_GROUPS.index(group) if group in STAT_GROUPS else len(STAT_GROUPS)
                    pe.wait_ge(std_ready.sem, std_ready.at(base, *STAT_GROUPS[n - 1]))
                pe.wait_ge(squared.sem, squared.at(base, *key))
                slot = sq_slot(key)
                col = 0 if key[0] == "r" else 4 * key[2]
                for b in range(BLK):
                    last = matmul(stat_bank[:, col + b:col + b + 1], sq[:, slot, b * P:(b + 1) * P], ones[:, 0:1],
                                  True, True)
                last.then_inc(stat_done.sem, 1)

            def turn(base, user):
                n = T_USERS.index(user)
                wait_turn_bank(pe, base, n)
                return turn_bank[n % 2]

            def score_target(base, user):
                n = S_USERS.index(user)
                if n >= 2:
                    pe.wait_ge(score_taken.sem, score_taken.at(base, *S_USERS[n - 2]))
                return score_bank[n % 2]

            for n in range(KT):
                stat(0, ("n", 0, n))
            with pe.Fori(0, DEPTH * STRIDE, STRIDE) as base:
                pe.get_value_cache().nocache = True
                for kind, *key in STEPS:
                    key = tuple(key)
                    if kind == "main":
                        main(base, *key)
                    elif kind == "stat":
                        stat(base, key)
                    elif kind == "bcast":
                        o = turn(base, (kind,) + key)
                        pe.wait_ge(rstd_ready.sem, rstd_ready.at(base, *rstd_of(key)))
                        col = 4 * key[2] if key[0] == "k" else 0
                        for b in range(BLK):
                            last = pe.transpose(o[:, b * P:(b + 1) * P],
                                                rs[:, col + b:col + b + 1].broadcast_to([P, P]), ident[:, :])
                        last.then_inc(bcast_done.sem, 1)
                    elif kind == "vtrans":
                        o = turn(base, (kind,) + key)
                        pe.wait_ge(stored_s.sem, stored_s.at(base, AT[key]))
                        for b in range(BLK):
                            last = pe.transpose(o[:, b * P:(b + 1) * P], vT[:, b * P:(b + 1) * P], ident[:, :])
                        last.then_inc(v_turned.sem, 1)
                    elif kind == "scores":
                        h, b = key
                        for c, (g, first, n) in enumerate(score_chunks(b)):
                            o = score_target(base, ("scores", h, b, c))
                            pe.wait_ge(k_scaled.sem, k_scaled.at(base, h, g))
                            matmul(o[:, 0:n * P], qk[g][:, b * P:(b + 1) * P], qk[3 + g][:, first * P:(first + n) * P],
                                   True, True).then_inc(scored.sem, 1)
                    elif kind == "ptrans":
                        h, b = key
                        pe.wait_ge(probs_ready.sem, probs_ready.at(base, h, b))
                        for c, (first, n) in enumerate(trans_chunks(b)):
                            o = turn(base, ("ptrans", h, b, c))
                            for j in range(n):
                                at = (SOFF[b] + first + j) * P
                                last = pe.transpose(o[:, j * P:(j + 1) * P], probs[:, at:at + P], ident[:, :])
                            last.then_inc(probs_turned.sem, 1)
                    elif kind == "pv":
                        h, b = key
                        if b == 0 and h > 0:
                            pe.wait_ge(low_ready.sem, low_ready.at(base, "yc", h - 1))
                        for g in range(N_GROUP):
                            pe.wait_ge(v_stored.sem, v_stored.at(base, "v", h, g))
                        pe.wait_ge(probsT_stored.sem, probsT_stored.at(base, h, b, len(trans_chunks(b)) - 1))
                        n = 0
                        for g, first, count in score_chunks(b):
                            for kb in range(first, first + count):
                                last = matmul(out_bank[:, b * P:(b + 1) * P], v_tok[g][:, kb, :],
                                              probsT[:, n * P:(n + 1) * P], n == 0, n == SBLK[b] - 1)
                                n += 1
                        last.then_inc(pv_done.sem, 1)
                    elif kind == "rscore":
                        h, m = key
                        o = score_target(base, ("rscore", h, m))
                        pe.wait_ge(stored_v.sem, stored_v.at(base, AT["rk", h]))
                        matmul(o[:, 0:SEQ - m * P], ret_k[:, m * P:(m + 1) * P], ret_q[:, m * P:SEQ],
                               True, True).then_inc(scored.sem, 1)
                    elif kind == "rpv":
                        h, = key
                        if h == 0:
                            pe.wait_ge(low_ready.sem, low_ready.at(base, "yc", HEADS - 1))
                        else:
                            pe.wait_ge(ret_copied.sem, ret_copied.at(base, h - 1))
                        pe.wait_ge(v_stored.sem, v_stored.at(base, "rv", h))
                        for m in range(BLK):
                            pe.wait_ge(score_taken.sem, score_taken.at(base, "rscore", h, m))
                            last = matmul(out_bank[:, m * P:SEQ], ret_v[:, m, :], ret_s[:, RS_OFF[m]:RS_OFF[m] + SEQ - m * P],
                                          m == 0, m == BLK - 1)
                        last.then_inc(ret_done.sem, 1)
                    elif kind == "fill_ahead":
                        close(pe, base, [stat_done])
                    elif kind == "mix":
                        g, = key
                        o = score_target(base, ("mix", g))
                        pe.wait_ge(ln_done.sem, ln_done.at(base, BLK - 1))
                        for b in range(BLK):
                            last = matmul(o[:, b * P:(b + 1) * P], sg_v[:, b, g * P:(g + 1) * P], sgw[:, g, :],
                                          True, True)
                        last.then_inc(scored.sem, 1)
                close(pe, base, [tile_done, bcast_done, v_turned, scored, probs_turned, pv_done,
                                 ret_done])

        @block.scalar
        def _(act):
            act.wait_ge(const_loaded, PRE_CONST)
            act.wait_ge(consts_set, 3)

            def split(base, *key):
                s = key[-1]
                raw_base = base + STRIDE if "next" in key else base
                act.wait_ge(raw_loaded[s % RAW_SLOTS].sem, raw_base + 16 * (s // RAW_SLOTS + 1))
                if "next" in key or s >= SPLIT_AHEAD:
                    if "next" in key or s >= PART_SLOTS:
                        act.wait_ge(slab_used.sem, slab_used.at(base, "slab", SLOT_BEFORE[s]))
                act.activation(w_high[:, PART_SLOT[s], :, :], raw[:, s % RAW_SLOTS, :, :], ACT.Copy).then_inc(
                    part_high_w.sem, 1)

            def square_x(base, w, n):
                key = ("n", w, n)
                before = ("n", 0, n - 2) if w == 0 else SQ_KEYS[SQ_KEYS.index(key) - 2]
                if w != 0 or n >= 2:
                    act.wait_ge(stat_done.sem, stat_done.at(base, *before))
                act.activation(sq[:, sq_slot(key), :], xT[:, n, :], ACT.Square).then_inc(squared.sem, 1)

            for s in range(SPLIT_AHEAD):
                split(0, s)
            for n in range(KT):
                act.wait_ge(x_loaded[n], 16)
                square_x(0, 0, n)
            with act.Fori(0, DEPTH * STRIDE, STRIDE) as base:
                act.get_value_cache().nocache = True
                act.wait_ge(layer_input, base + 1)
                for kind, *key in STEPS:
                    key = tuple(key)
                    if kind == "split":
                        split(base, *key)
                    elif kind == "fill_ahead":
                        close(act, base, [squared])
                    elif kind == "fill_split":
                        close(act, base, [part_high_w])
                    elif kind == "load_sqrt":
                        act.activation(sqrt_out[:, :], eps[:, :], ACT.Sqrt).then_inc(sqrt_loaded.sem, 1)
                    elif kind == "evac":
                        i, = key
                        t = TILES[i]
                        if t[0] not in EVAC_BY_SCALAR:
                            continue
                        act.wait_ge(tile_done.sem, tile_done.at(base, i))
                        src = main_bank[i % 2][:, :]
                        if t[0] in ("v", "rv", "sv"):
                            order = keys("vtrans")
                            n = order.index(t)
                            if n > 0:
                                act.wait_ge(v_turned.sem, v_turned.at(base, *order[n - 1]))
                            dst, func = vT[:, :], ACT.Gelu_apprx_tanh if t[0] == "sv" else ACT.Copy
                        elif t[0] == "rg":
                            if t[1] > 1:
                                act.wait_ge(product.sem, product.at(base, "yr", t[1] - 2))
                            dst, func = ret_g[t[1] % 2], ACT.Silu
                        elif t[0] == "su":
                            dst, func = sg_u[t[1]], ACT.Gelu_apprx_tanh
                        else:
                            n = GATE_TILES.index(i)
                            dst, func = gates[n % 2], ACT.Sigmoid if t[0] == "gate" else ACT.Silu
                            if n >= 2:
                                u = TILES[GATE_TILES[n - 2]]
                                j = AT["proj" if u[0] == "gate" else "fup", u[1], u[2]]
                                act.wait_ge(stored_v.sem, stored_v.at(base, j))
                        act.activation(dst, src, func).then_inc(stored_s.sem, 1)
                    elif kind == "square" and key[0] == "n":
                        tile = AT["wo", key[2]] if key[1] == 1 else AT["down", 1, key[2]]
                        act.wait_ge(stored_v.sem, stored_v.at(base, tile))
                        square_x(base, *key[1:])
                    elif kind == "square":
                        n = SQ_KEYS.index(key)
                        if n >= 2:
                            act.wait_ge(stat_done.sem, stat_done.at(base, *SQ_KEYS[n - 2]))
                        if key[0] == "r":
                            src = ret_y[:, :]
                            act.wait_ge(ret_copied.sem, ret_copied.at(base, key[1]))
                        else:
                            src = qk[key[2] + (3 if key[0] == "ck" else 0)]
                            act.wait_ge(stored_v.sem, stored_v.at(base, AT[key[0][1], key[1], key[2]]))
                        act.activation(sq[:, n % 2, :], src, ACT.Square).then_inc(squared.sem, 1)
                    elif kind == "rstd":
                        n = STAT_GROUPS.index(key)
                        if n > 0:
                            act.wait_ge(rstd_ready.sem, rstd_ready.at(base, *STAT_GROUPS[n - 1]))
                        if key[0] == "n":
                            act.wait_ge(norm_summed.sem, norm_summed.at(base, *key))
                            src, cols, width = nsum[:, :], BLK, D_MODEL
                        else:
                            act.wait_ge(stat_done.sem, stat_done.at(base, *([k for k in keys("stat") if k[:2] == key][-1])))
                            cols, width = (BLK if key[0] == "r" else N_GROUP * BLK), P
                            src = stat_bank[:, 0:cols]
                        act.activation(std[:, 0:cols], src, ACT.Sqrt, bias=(eps_q if key[0] == "cq" else eps)[:, 0:1],
                                       scale=1.0 if key[0] == "cq" else 1.0 / width).then_inc(std_ready.sem, 1)
                    elif kind == "high":
                        if key[0] == "yc":
                            act.wait_ge(pv_done.sem, pv_done.at(base, key[1], BLK - 1))
                            src = out_bank[:, :]
                        else:
                            act.wait_ge(product.sem, product.at(base, *key))
                            src = prod[:, PROD_KEYS.index(key) % 2, :]
                        act.activation(parts(key)[0], src, ACT.Copy).then_inc(high_ready.sem, 1)
                    elif kind == "vtrans":
                        act.wait_ge(v_turned.sem, v_turned.at(base, *key))
                        src = turn_bank[T_USERS.index((kind,) + key) % 2][:, :].rearrange("p (b e) -> p b e", b=BLK)
                        if key[0] == "v":
                            dst = v_tok[key[2]]
                        elif key[0] == "rv":
                            dst = ret_v[:, :, :]
                        else:
                            dst = sg_v[:, :, key[1] * P:(key[1] + 1) * P]
                        act.activation(dst, src, ACT.Copy).then_inc(v_stored.sem, 1)
                    elif kind == "softmax":
                        h, b = key
                        act.wait_ge(max_ready.sem, max_ready.at(base, h, b))
                        at = SOFF[b] * P
                        for g, _, n in score_chunks(b):
                            e = act.activation(probs[:, at:at + n * P], probs[:, at:at + n * P], ACT.Exp,
                                               bias=negm[:, b:b + 1], scale=crow[:, g, b:b + 1],
                                               accum_out=den[:, b, g:g + 1])
                            at += n * P
                        e.then_inc(exp_ready.sem, 1)
                    elif kind == "ptrans":
                        h, b = key
                        if b > 0:
                            act.wait_ge(pv_done.sem, pv_done.at(base, h, b - 1))
                        for c, (first, n) in enumerate(trans_chunks(b)):
                            act.wait_ge(probs_turned.sem, probs_turned.at(base, h, b, c))
                            src = turn_bank[T_USERS.index(("ptrans", h, b, c)) % 2][:, 0:n * P]
                            act.activation(probsT[:, first * P:(first + n) * P], src, ACT.Copy).then_inc(
                                probsT_stored.sem, 1)
                    elif kind == "ocopy":
                        h, = key
                        act.wait_ge(ret_done.sem, ret_done.at(base, h))
                        if h > 0:
                            act.wait_ge(product.sem, product.at(base, "yr", h - 1))
                        act.activation(ret_y[:, :], out_bank[:, :], ACT.Copy).then_inc(ret_copied.sem, 1)
                    elif kind == "ln" and key == (0,):
                        act.wait_ge(ln_var.sem, ln_var.at(base))
                        act.activation(lnstd[:, :], mv[:, :, 1], ACT.Sqrt, bias=eps[:, 0:1]).then_inc(ln_std.sem, 1)
                close(act, base, [stored_s, sqrt_loaded, std_ready, high_ready, v_stored, exp_ready,
                                  probsT_stored, ret_copied, ln_std])

        @block.vector
        def _(dve):
            dve.memset(ones[:, :], 1.0).then_inc(consts_set, 1)
            dve.memset(eps[:, :], EPS).then_inc(consts_set, 1)
            dve.memset(eps_q[:, :], EPS * P).then_inc(consts_set, 1)
            dve.wait_ge(const_loaded, PRE_CONST)
            dve.wait_ge(consts_set, 3)
            dve.sem_inc(layer_input, 1)

            def split(base, *key):
                s = key[-1]
                dve.wait_ge(part_high_w.sem, part_high_w.at(base, *key))
                dve.tensor_tensor(w_low[:, PART_SLOT[s], :, :], raw[:, s % RAW_SLOTS, :, :],
                                  w_high[:, PART_SLOT[s], :, :], ALU.subtract).then_inc(part_low_w.sem, 1)

            for s in range(SPLIT_AHEAD):
                split(0, s)
            with dve.Fori(0, DEPTH * STRIDE, STRIDE) as base:
                dve.get_value_cache().nocache = True
                chained = [0]

                def chain(ins):
                    ins.then_inc(vector_chain, 1)
                    chained[0] += 1
                    dve.wait_ge(vector_chain, base + chained[0])

                def product_slot(key):
                    n = PROD_KEYS.index(key)
                    if n >= 2:
                        dve.wait_ge(low_ready.sem, low_ready.at(base, *PROD_KEYS[n - 2]))
                    return prod[:, n % 2, :]

                tmp_read = []

                def tmp_free():
                    if tmp_read:
                        sig, key = tmp_read[-1]
                        dve.wait_ge(sig.sem, sig.at(base, *key))

                dve.wait_ge(vec_loaded, base + 16)
                chain(dve.tensor_tensor(gqk[:, :], vec[:, 20:21], vec[:, 21:22], ALU.mult))
                for kind, *key in STEPS:
                    key = tuple(key)
                    if kind == "split":
                        split(base, *key)
                    elif kind == "fill_split":
                        close(dve, base, [part_low_w])
                    elif kind == "evac":
                        i, = key
                        t = TILES[i]
                        if t[0] in EVAC_BY_SCALAR:
                            continue
                        dve.wait_ge(tile_done.sem, tile_done.at(base, i))
                        src = main_bank[i % 2][:, :]
                        if t[0] in ("q", "k"):
                            dve.tensor_copy(qk[t[2] + (3 if t[0] == "k" else 0)], src).then_inc(stored_v.sem, 1)
                        elif t[0] in ("rq", "rk"):
                            dst = ret_q if t[0] == "rq" else ret_k
                            half = P // 2
                            tmp_free()
                            dve.tensor_tensor(dst, src, rot[:, 0, :], ALU.mult)
                            dve.tensor_tensor(tmp[0:half, :], main_bank[i % 2][half:P, :], rot[half:P, 1, :], ALU.mult)
                            chain(dve.tensor_tensor(tmp[half:P, :], main_bank[i % 2][0:half, :], rot[0:half, 1, :], ALU.mult))
                            dve.tensor_tensor(dst, dst, tmp[:, :], ALU.add).then_inc(stored_v.sem, 1)
                            tmp_read.append((stored_v, (i,)))
                        elif t[0] == "proj":
                            _, br, n = t
                            dve.wait_ge(stored_s.sem, stored_s.at(base, AT["gate", br, n]))
                            g = gates[GATE_TILES.index(AT["gate", br, n]) % 2]
                            if br == 2:
                                dve.tensor_tensor(merged[n], src, g, ALU.mult).then_inc(stored_v.sem, 1)
                            else:
                                tmp_free()
                                chain(dve.tensor_tensor(tmp[:, :], src, g, ALU.mult))
                                tmp_read.append((stored_v, (i,)))
                                if br == 0:
                                    dve.tensor_tensor(merged[n], merged[n], tmp[:, :], ALU.add).then_inc(stored_v.sem, 1)
                                else:
                                    dst = product_slot(("m", n))
                                    chain(dve.tensor_tensor(dst, merged[n], tmp[:, :], ALU.add))
                                    dve.sem_inc(product.sem, 1)
                                    dve.sem_inc(stored_v.sem, 1)
                        elif t[0] in ("wo", "down"):
                            dve.tensor_tensor(xT[:, t[-1], :], src, xT[:, t[-1], :], ALU.add).then_inc(stored_v.sem, 1)
                        else:
                            g = AT["fgate", t[1], t[2]]
                            dve.wait_ge(stored_s.sem, stored_s.at(base, g))
                            dst = product_slot(("f", t[1], t[2]))
                            chain(dve.tensor_tensor(dst, src, gates[GATE_TILES.index(g) % 2], ALU.mult))
                            dve.sem_inc(product.sem, 1)
                            dve.sem_inc(stored_v.sem, 1)
                    elif kind == "low":
                        dve.wait_ge(high_ready.sem, high_ready.at(base, *key))
                        hi, lo = parts(key)
                        src = out_bank[:, :] if key[0] == "yc" else prod[:, PROD_KEYS.index(key) % 2, :]
                        dve.tensor_tensor(lo, src, hi, ALU.subtract).then_inc(low_ready.sem, 1)
                    elif kind == "rstd":
                        if key[0] == "n":
                            dve.wait_ge(stat_done.sem, stat_done.at(base, "n", key[1], KT - 1))
                            dve.tensor_reduce(nsum[:, :], stat_bank[:, 0:4 * KT].rearrange("p (n b) -> p b n", b=BLK),
                                              AX_X, ALU.add).then_inc(norm_summed.sem, 1)
                        dve.wait_ge(std_ready.sem, std_ready.at(base, *key))
                        if key[0] == "cq":
                            if key[1] > 0:
                                dve.wait_ge(exp_ready.sem, exp_ready.at(base, key[1] - 1, BLK - 1))
                            dve.reciprocal(crow[:, :, :].rearrange("p g b -> p (g b)"), std[:, :]).then_inc(
                                rstd_ready.sem, 1)
                        else:
                            order = keys("bcast")
                            first = order.index(("k", key[1], 0) if key[0] == "ck" else key)
                            if first > 0:
                                dve.wait_ge(bcast_done.sem, bcast_done.at(base, *order[first - 1]))
                            cols = N_GROUP * BLK if key[0] == "ck" else BLK
                            dve.reciprocal(rs[:, 0:cols], std[:, 0:cols]).then_inc(rstd_ready.sem, 1)
                    elif kind == "hprod":
                        w, n = key
                        dve.wait_ge(bcast_done.sem, bcast_done.at(base, "n", w))
                        dst = product_slot(("h", w, n))
                        dve.scalar_tensor_tensor(dst, xT[:, n, :], vec[:, 8 * w + n:8 * w + n + 1],
                                                 turn_bank[T_USERS.index(("bcast", "n", w)) % 2][:, :],
                                                 ALU.mult, ALU.mult).then_inc(product.sem, 1)
                    elif kind == "kscale":
                        h, g = key
                        dve.wait_ge(bcast_done.sem, bcast_done.at(base, "k", h, g))
                        dve.wait_ge(squared.sem, squared.at(base, "ck", h, g))
                        dve.scalar_tensor_tensor(qk[3 + g], qk[3 + g], gqk[:, 0:1],
                                                 turn_bank[T_USERS.index(("bcast", "k", h, g)) % 2][:, :],
                                                 ALU.mult, ALU.mult).then_inc(k_scaled.sem, 1)
                    elif kind == "scores":
                        h, b = key
                        at = SOFF[b] * P
                        for c, (g, _, n) in enumerate(score_chunks(b)):
                            m = (2 - n) if g == 0 else 2 + 4 * (g - 1) + 4 - n
                            dve.wait_ge(scored.sem, scored.at(base, "scores", h, b, c))
                            own_wait(dve)
                            dve.tensor_tensor_reduce(probs[:, at:at + n * P],
                                                     score_bank[S_USERS.index(("scores", h, b, c)) % 2][:, 0:n * P],
                                                     mask[:, m:m + n, :].rearrange("p a n -> p (a n)"), 1.0, -3e38,
                                                     ALU.add, ALU.max, smax[:, b, g:g + 1]).then_inc(score_taken.sem, 1)
                            at += n * P
                        dve.wait_ge(score_taken.sem, score_taken.at(base, "scores", h, b, 2))
                        dve.wait_ge(rstd_ready.sem, rstd_ready.at(base, "cq", h))
                        chain(dve.tensor_tensor(smax2[:, b, :], smax[:, b, :], crow[:, :, b], ALU.mult))
                        dve.tensor_reduce(negm[:, b:b + 1], smax2[:, b, :], AX_X, ALU.max, negate=True).then_inc(
                            max_ready.sem, 1)
                    elif kind == "softmax":
                        h, b = key
                        dve.wait_ge(exp_ready.sem, exp_ready.at(base, h, b))
                        chain(dve.tensor_reduce(dsum[:, b:b + 1], den[:, b, :], AX_X, ALU.add))
                        chain(dve.reciprocal(rden[:, b:b + 1], dsum[:, b:b + 1]))
                        p = probs[:, SOFF[b] * P:(SOFF[b] + SBLK[b]) * P]
                        dve.tensor_scalar(p, p, rden[:, b:b + 1], None, ALU.mult).then_inc(probs_ready.sem, 1)
                    elif kind == "rscore":
                        h, m = key
                        n = SEQ - m * P
                        dve.wait_ge(scored.sem, scored.at(base, "rscore", h, m))
                        dve.wait_ge(decay_loaded[h % 2], base + 16 * (h // 2 + 1))
                        dve.tensor_tensor(ret_s[:, RS_OFF[m]:RS_OFF[m] + n],
                                          score_bank[S_USERS.index(("rscore", h, m)) % 2][:, 0:n],
                                          decay_sb[:, h % 2, 0:n], ALU.mult).then_inc(score_taken.sem, 1)
                    elif kind == "rscale":
                        h, = key
                        dve.wait_ge(bcast_done.sem, bcast_done.at(base, "r", h))
                        dve.wait_ge(squared.sem, squared.at(base, "r", h))
                        dve.wait_ge(stored_s.sem, stored_s.at(base, AT["rg", h]))
                        dst = product_slot(("yr", h))
                        tmp_free()
                        tmp_read.append((product, ("yr", h)))
                        chain(dve.scalar_tensor_tensor(tmp[:, :], ret_y[:, :], vec[:, 16 + h:17 + h],
                                                       turn_bank[T_USERS.index(("bcast", "r", h)) % 2][:, :],
                                                       ALU.mult, ALU.mult))
                        dve.tensor_tensor(dst, tmp[:, :], ret_g[h % 2], ALU.mult).then_inc(product.sem, 1)
                    elif kind == "ln":
                        step, = key
                        if step == 0:
                            dve.wait_ge(spatial_loaded, base + 32)
                            chain(dve.tensor_tensor(sgw[:, :, :], sgw[:, :, :],
                                                    mask[:, 10:11, :].broadcast_to([P, HEADS, P]), ALU.mult))
                            for c in range(HEADS):
                                dve.wait_ge(v_stored.sem, v_stored.at(base, "sv", c))
                            for b in range(BLK):
                                last = dve.bn_stats(bn6[:, b, :], sg_v[:, b, :])
                            chain(last)
                            own_wait(dve)
                            for b in range(BLK):
                                last = dve.bn_aggr(mv[:, b, :], bn6[:, b, :])
                            last.then_inc(ln_var.sem, 1)
                            dve.wait_ge(ln_std.sem, ln_std.at(base))
                            chain(dve.reciprocal(lnrs[:, :], lnstd[:, :]))
                        v = sg_v[:, step, :]
                        chain(dve.tensor_scalar(v, v, mv[:, step, 0:1], lnrs[:, step:step + 1],
                                                ALU.subtract, ALU.mult))
                        chain(dve.tensor_tensor(v, v, row[:, 0, :], ALU.mult))
                        dve.tensor_tensor(v, v, row[:, 1, :], ALU.add).then_inc(ln_done.sem, 1)
                    elif kind == "mix":
                        g, = key
                        dve.wait_ge(scored.sem, scored.at(base, "mix", g))
                        dve.wait_ge(stored_s.sem, stored_s.at(base, AT["su", g]))
                        dst = product_slot(("ys", g))
                        src = score_bank[S_USERS.index(("mix", g)) % 2][:, :].rearrange("p (b n) -> p b n", b=BLK)
                        tmp_free()
                        tmp_read.append((product, ("ys", g)))
                        ins = dve.tensor_tensor(tmp[:, :].rearrange("p (b n) -> p b n", b=BLK), src,
                                                row[:, 2:3, g * P:(g + 1) * P].broadcast_to([P, BLK, P]), ALU.add)
                        ins.then_inc(score_taken.sem, 1)
                        dve.wait_ge(score_taken.sem, score_taken.at(base, "mix", g))
                        dve.tensor_tensor(dst, tmp[:, :], sg_u[g], ALU.mult).then_inc(product.sem, 1)
                close(dve, base, [stored_v, norm_summed, rstd_ready, product, low_ready,
                                  k_scaled, score_taken, max_ready, probs_ready, ln_var, ln_done])
                dve.wait_ge(vector_chain, base + chained[0])
                dve.sem_inc(vector_chain, STRIDE - chained[0])
                dve.sem_inc(layer_input, STRIDE)



def _columns():
    ka, va, ga, ub, vb = 512, 1024, 1536, 2048, 2560
    qc = 3072
    kc, vc, gates = qc + 1536, qc + 3072, qc + 4608

    def of(t):
        if t[0] in "qkv":
            return {"q": qc, "k": kc, "v": vc}[t[0]] + t[2] * 512 + t[1] * P
        if t[0] == "gate":
            return gates + t[1] * D_MODEL + t[2] * P
        return {"rq": 0, "rk": ka, "rv": va, "rg": ga, "su": ub, "sv": vb}[t[0]] + t[1] * P
    return of


def _weights(w_in, w_branch, w_o, w_gate_up, w_down):
    of = _columns()
    out = np.empty((DEPTH * SLABS + RAW_SLOTS, P, 8, P), np.float32)
    for layer in range(DEPTH):
        for t, blocks in zip(TILES, BLOCKS):
            if t[0] == "proj":
                src, col, row0 = w_branch[layer, t[1]], t[2] * P, 0
            elif t[0] == "wo":
                src, col, row0 = w_o[layer], t[1] * P, 0
            elif t[0] in ("fgate", "fup"):
                src, col, row0 = w_gate_up[layer], (D_FF if t[0] == "fup" else 0) + (t[1] * FF_HALF + t[2]) * P, 0
            elif t[0] == "down":
                src, col, row0 = w_down[layer], t[2] * P, t[1] * FF_HALF * P
            else:
                src, col, row0 = w_in[layer], of(t), 0
            for s, place, k in blocks:
                r = row0 + k * P
                out[layer * SLABS + s, :, place, :] = src[r:r + P, col:col + P]
    out[DEPTH * SLABS:] = out[:RAW_SLOTS]
    return out.reshape(-1, P, 8 * P)


def _constants():
    f = np.float32
    half = P // 2
    inv = (f(1.0) / (f(ROPE_BASE) ** (np.arange(half, dtype=f) / f(half)))).astype(f)
    ang = (np.arange(SEQ, dtype=f)[:, None] * inv[None, :]).astype(f)
    cos, sin = np.cos(ang).T.astype(f), np.sin(ang).T.astype(f)
    rotation = np.stack([np.concatenate([cos, cos]), np.concatenate([sin, -sin])], axis=1)
    log_g = np.log1p(-(2.0 ** (-5.0 - np.arange(HEADS))))
    dist = np.arange(SEQ)[None, :] - np.arange(P)[:, None]
    decay = np.where(dist[None] >= 0, np.exp(log_g[:, None, None] * np.maximum(dist, 0)) * SCALE, 0.0).astype(f)
    q, k = np.arange(P)[:, None], np.arange(P)[None, :]
    causal = k <= q
    blocks = [(q + P - k) <= DILATIONS[0][0], causal]
    for _, d in DILATIONS[1:]:
        same = (q - k) % d == 0
        blocks += [same] * 3 + [same & causal]
    masks = [np.where(b, 0.0, NEG) for b in blocks] + [np.where(q <= k, 1.0, 0.0)]
    masks = (np.stack(masks, axis=1).astype(f).view(np.uint32) >> 16).astype(np.uint16)
    return rotation.astype(f), decay, masks, np.eye(P, dtype=f)


def kernel(x, g_mix, w_in, ret_norm_g, sg_ln_g, sg_ln_b, sg_w, sg_b, dil_q_norm_g, dil_k_norm_g, w_branch, w_o,
           g_ffn, w_gate_up, w_down):
    import concourse.bacc as bacc
    from concourse.bass_utils import run_bass_kernel_spmd

    def per_layer(a, n):
        return np.asarray(a).reshape(DEPTH, n, P).transpose(0, 2, 1)

    def and_again(a):
        return np.ascontiguousarray(np.concatenate([a, a[-1:]]))

    rotation, decay, masks, ident = _constants()
    arrays = {
        "x_t": np.ascontiguousarray(np.asarray(x)[0].T.reshape(KT, P, SEQ).transpose(1, 0, 2)),
        "weights": _weights(*(np.asarray(a) for a in (w_in, w_branch, w_o, w_gate_up, w_down))),
        "vecs": and_again(np.concatenate([per_layer(g_mix, KT), per_layer(g_ffn, KT), per_layer(ret_norm_g, HEADS),
                                          per_layer(dil_q_norm_g, 1), per_layer(dil_k_norm_g, 1)], axis=2)),
        "spatial": and_again(np.asarray(sg_w).transpose(0, 3, 1, 2)),
        "rows": and_again(np.stack([np.asarray(sg_ln_g), np.asarray(sg_ln_b), np.asarray(sg_b).reshape(DEPTH, -1)],
                                   axis=1)),
        "rotation": rotation, "decay": decay, "masks": masks, "ident": ident,
    }
    nc = bacc.Bacc("TRN2", target_bir_lowering=False, num_devices=1)
    aps = [nc.dram_tensor(name, a.shape, mybir.dt.from_np(a.dtype), kind="ExternalInput").ap()
           for name, a in arrays.items()]
    out = nc.dram_tensor("out_t", (P, KT, SEQ), F32, kind="ExternalOutput").ap()
    build(nc, *aps, out)
    r = run_bass_kernel_spmd(nc, [arrays], core_ids=[0])
    y = r.results[0]["out_t"]
    return np.ascontiguousarray(y.transpose(2, 1, 0).reshape(1, SEQ, D_MODEL))
```

```python
from contextlib import ExitStack

import numpy as np

import concourse.bass as bass
from concourse import mybir

P = 128
D_MODEL = 1024
SEQ = 512
DEPTH = 2
EPS = 1e-6
HEADS = 4
N_GROUP = 3
D_FF = 2816
KT = D_MODEL // P
BLK = SEQ // P
FF_HALF = D_FF // P // 2
DILATIONS = ((128, 1), (512, 4), (2048, 16))
ROPE_BASE = 10000.0
NEG = -1e30
SCALE = float(P) ** -0.5

RAW_SLOTS = 3
PART_SLOTS = 3

ALU = mybir.AluOpType
ACT = mybir.ActivationFunctionType
AX_X = mybir.AxisListType.X
F32 = mybir.dt.float32
F32R = mybir.dt.float32r
BF16 = mybir.dt.bfloat16



def tiles_of_layer():
    t = []
    for h in range(HEADS):
        t += [("k", h, g) for g in range(N_GROUP)] + [("q", h, g) for g in range(N_GROUP)]
        t += [("v", h, g) for g in range(N_GROUP)]
    for h in range(HEADS):
        t += [("rq", h), ("rk", h), ("rv", h), ("rg", h)]

    def gated(branch):
        out = []
        for n in range(0, KT, 2):
            out += [("gate", branch, n), ("gate", branch, n + 1), ("proj", branch, n), ("proj", branch, n + 1)]
        return out

    t += gated(2)
    t += [("sv", c) for c in range(HEADS)] + [("su", c) for c in range(HEADS)]
    t += gated(0) + gated(1)
    t += [("wo", n) for n in range(KT)]
    for half in range(2):
        for j in range(FF_HALF):
            t += [("fgate", half, j), ("fup", half, j)]
        t += [("down", half, n) for n in range(KT)]
    return t


TILES = tiles_of_layer()
AT = {t: i for i, t in enumerate(TILES)}


def blocks_of_tiles():
    out, n = [], 0
    for t in TILES:
        k = 4 if t[0] == "proj" else FF_HALF if t[0] == "down" else KT
        out.append([((n + i) // 8, (n + i) % 8, i) for i in range(k)])
        n += k
    assert n % 8 == 0
    return out, n // 8


BLOCKS, SLABS = blocks_of_tiles()
STRIDE = 16 * SLABS
FIRST_USE = {s: min(i for i, b in enumerate(BLOCKS) if any(x[0] == s for x in b)) for s in range(SLABS)}
LAST_BLOCK = {b[0]: (i, b) for i, bs in enumerate(BLOCKS) for b in bs}
PART_SLOT = [s % PART_SLOTS for s in range(SLABS - PART_SLOTS)] + list(range(PART_SLOTS))
SLOT_BEFORE = [next((u for u in range(s - 1, -1, -1) if PART_SLOT[u] == PART_SLOT[s]), SLABS - PART_SLOTS + s)
               for s in range(SLABS)]
SPLIT_AHEAD = 2

PROJECTION_EVENTS = []
for _i, _bs in enumerate(BLOCKS):
    PROJECTION_EVENTS += [("slab", b[0]) for b in _bs[:-1] if LAST_BLOCK[b[0]] == (_i, b)] + [(_i,)]

SCALED_ROLES = {"rq", "rk", "v", "rv", "sv", "rg", "su", "gate", "fgate"}
ACTIVATED_ROLES = {"sv", "rg", "su", "gate", "fgate"}


PHASES = 4
assert DILATIONS[0] == (P, 1) and SEQ == PHASES * P
assert all(d % PHASES == 0 and w >= SEQ for w, d in DILATIONS[1:])
SCORE_BLOCKS = [(0, b, kb) for b in range(BLK) for kb in range(max(b - 1, 0), b + 1)]
SCORE_BLOCKS += [(g, r, r) for g in range(1, N_GROUP) for r in range(PHASES)]
UNIT_OF_GROUP = {0: (0, 1), 1: (2,), 2: (3,)}
UNITS = [[n for n, (g, b, _) in enumerate(SCORE_BLOCKS) if UNIT_OF_GROUP[g][b // 2 if g == 0 else 0] == u]
         for u in range(4)]


def rows_of_unit(u):
    out = []
    for n in UNITS[u]:
        g, b, _ = SCORE_BLOCKS[n]
        if out and out[-1][:2] == (g, b):
            out[-1] = (g, b, out[-1][2], out[-1][3] + 1)
        else:
            out.append((g, b, n, 1))
    return out


def mask_of(g, n):
    return {0: 2 - n, 1: 1, 2: 2}[g]


SPATIAL_MASK = 3


def schedule():
    pre = {i: [] for i in range(len(TILES))}
    post = {i: [] for i in range(len(TILES))}
    for h in range(HEADS):
        t = AT["k", h, 0]
        for j in range(N_GROUP):
            post[t + j] += [("square", "ck", h, j), ("split_sq", "ck", h, j)]
            pre[t + (1, 4, 4)[j]] += [("rowstat", "ck", h, j), ("rowstd", "ck", h, j)]
            post[t + 3 + j] += [("rowinv", "ck", h, j), ("rowscale", "ck", h, j)]
            post[t + 3 + j] += [("square", "cq", h, j)]
            pre[t + 4 + j] += [("stat", "cq", h, j)]
            if j > 0:
                pre[t + 7 + j] += [("vtrans", "v", h, j)]
        pre[t + 6] += [("rstd", "cq", h)]
        pre[t + 7] += [("scores", h, 0), ("scores", h, 1), ("expo", h, 0), ("vtrans", "v", h, 0)]
        pre[t + 8] += [("scores", h, 2), ("scores", h, 3), ("expo", h, 1)]
        post[t + 8] += [("gather", h), ("swap", h)]
        if h < HEADS - 1:
            pre[t + 10] += [("weigh", h)]
        pre[t + 11] += [("ptrans", h, 0), ("ptrans", h, 1)]
        pre[t + 12] += [("ptrans", h, 2), ("pv", h, 0), ("ptrans", h, 3)]
        pre[t + 13] += [("pv", h, 1), ("pv", h, 2), ("high", "yc", h), ("low", "yc", h)]
    for h in range(HEADS):
        t = AT["rq", h]
        post[t] += [("rotate", "rq", h)]
        if h == 0:
            post[t] += [("weigh", HEADS - 1)]
        post[t + 1] += [("rotate", "rk", h)]
        pre[t + 3] += [("vtrans", "rv", h)] + [("rscore", h, m) for m in range(2)]
        pre[t + 4] += [("rscore", h, m) for m in range(2, BLK)]
        pre[t + 5] += [("rpv", h), ("ocopy", h), ("square", "r", h), ("split_sq", "r", h)]
        pre[t + 6] += [("rowstat", "r", h), ("rowstd", "r", h)]
        post[t + 6] += [("rowinv", "r", h)]
        post[t + 7 + (h == HEADS - 1)] += [("rowscale", "r", h), ("high", "yr", h), ("low", "yr", h)]
    t = AT["sv", 0]
    for c in range(HEADS):
        pre[t + c + 1] += [("vtrans", "sv", c)]
    post[t + 4] += [("lnvar",)]
    for b in range(BLK):
        post[t + 5 + b] += [("ln", b)]
    for g in range(HEADS):
        post[AT["gate", 0, 2 + 2 * g] if g < 3 else AT["gate", 1, 0]] += [("mix", g), ("high", "ys", g), ("low", "ys", g)]
    for n in range(KT):
        post[AT["proj", 1, n]] += [("high", "m", n), ("low", "m", n)]
        for tile, which in ((AT["wo", n], 1), (AT["down", 1, n], "next")):
            post[tile] += [("high", "h", which, n), ("low", "h", which, n), ("square", "n", which, n)]
            if n > 0:
                post[tile] += [("sumsq", "n", which, n)]
            if n == KT - 1:
                pre[tile] += [("load_sqrt",)]
    for half in range(2):
        for j in range(FF_HALF):
            post[AT["fup", half, j]] += [("high", "f", half, j), ("low", "f", half, j)]

    post[AT["down", 1, KT - 2]] += [("fill_split",), ("split_high", "next", 0), ("split_low", "next", 0)]
    pre[AT["down", 1, KT - 1]] += [("split_high", "next", 1), ("split_low", "next", 1)]
    pre[AT["down", 1, 0]] = [("fill_ahead",)] + pre[AT["down", 1, 0]]

    steps, split = [], SPLIT_AHEAD
    for i in range(len(TILES)):
        if i in AFTER_NORM:
            w = AFTER_NORM.index(i)
            steps += [("main", i, 0, NORM_AT), ("stat", "n", w), ("rstd", "n", w), ("main", i, NORM_AT, KT),
                      ("bcast", "n", w), ("keep_rstd", w)]
        else:
            steps.append(("main", i, 0, len(BLOCKS[i])))
        todo = []
        while split < PART_SLOTS or (split < SLABS and FIRST_USE[split - PART_SLOTS + 1] <= i + 1
                                     and LAST_BLOCK[SLOT_BEFORE[split]][0] <= i):
            todo.append(split)
            split += 1
        for s in todo:
            steps.append(("split_high", s))
            if FIRST_USE[s] <= i:
                steps.append(("split_low", s))
        steps += pre[i] + [("evac", i)] + [("split_low", s) for s in todo if FIRST_USE[s] > i] + post[i]
    assert split == SLABS
    return steps


NORM_AT = KT - 2
AFTER_NORM = (AT["k", 0, 0], AT["fgate", 0, 0])
STEPS = schedule()


def keys(kind, *starts):
    return [s[1:] for s in STEPS if s[0] == kind and (not starts or s[1] in starts)]


class Signal:

    def __init__(self, sem, events, ahead=()):
        self.sem = sem
        events = [k for k in events if "next" not in k]
        self.number = {k: i + 1 for i, k in enumerate(list(ahead) + events)}
        self.count = len(events)
        self.ahead = len(ahead)
        assert len(self.number) == len(events) + len(ahead) < STRIDE

    def at(self, base, *key):
        if "next" in key:
            key = key[1:] if key[0] == "next" else tuple(0 if k == "next" else k for k in key)
            return base + STRIDE + self.number[key]
        return base + self.number[key]


T_USERS = []
for _s in STEPS:
    if _s[0] in ("bcast", "rowstat", "vtrans", "ptrans"):
        T_USERS.append(_s)
S_USERS = []
for _s in STEPS:
    if _s[0] in ("scores", "rscore", "mix"):
        S_USERS.append(_s)
SQ_KEYS = keys("square")
SCALED_TILES = [t for t in TILES if t[0] in SCALED_ROLES]
STAT_GROUPS = keys("rstd")
ROW_KEYS = keys("rowstat")
PROD_KEYS = [s[1:] for s in STEPS if s[0] == "high" and s[1] not in ("yc", "h")]
GATE_TILES = [i for i, t in enumerate(TILES) if t[0] in ("gate", "fgate")]


def build(nc, x_in, weights, gain_first, vecs, spatial, rows, rotation, decay, masks, ident_in, pairs_dram, out):
    with ExitStack() as ctx:
        def sb(name, shape, dt=F32):
            return ctx.enter_context(nc.sbuf_tensor(name, shape, dt))

        def signal(name, events, ahead=()):
            return Signal(ctx.enter_context(nc.semaphore(name)), events, ahead)

        raw = sb("raw", [P, RAW_SLOTS, 8, P])
        w_high = sb("w_high", [P, PART_SLOTS, 8, P], F32R)
        w_low = sb("w_low", [P, PART_SLOTS, 8, P], F32R)
        xT = sb("xT", [P, KT, SEQ])
        h_high = sb("h_high", [P, KT, SEQ], F32R)
        h_low = sb("h_low", [P, KT, SEQ], F32R)
        in_high = sb("in_high", [P, 12, SEQ], F32R)
        in_low = sb("in_low", [P, 12, SEQ], F32R)
        work = sb("work", [P, 19, SEQ])
        ret_v = sb("ret_v", [P, BLK, P])
        tmp = sb("tmp", [P, SEQ])
        prod = sb("prod", [P, 2, SEQ])
        sq = sb("sq", [P, 2, SEQ])
        scaled = sb("scaled", [P, 2, SEQ])
        norm_rstd = sb("norm_rstd", [P, SEQ])
        decay_sb = sb("decay_sb", [P, SEQ])
        rot = sb("rot", [P, 2, SEQ])
        mask_bits = sb("mask_bits", [P, 4, P], mybir.dt.uint16)
        mask = mask_bits[:, :, :].bitcast(BF16)
        ident = sb("identity", [P, P])
        ones = sb("ones", [P, P])
        ones_r = sb("ones_r", [P, P], F32R)
        vec = sb("vec", [P, 22])
        sgw = sb("sgw", [P, HEADS, P])
        row = sb("row", [P, 3, SEQ])
        eps = sb("eps", [P, 1])
        eps_q = sb("eps_q", [P, 1])
        sqrt_out = sb("sqrt_out", [P, 1])
        gqk = sb("gqk", [P, 1])
        first_gain = sb("first_gain", [P, KT])
        std = sb("std", [P, N_GROUP * BLK])
        rs = sb("rs", [P, BLK])
        crow = sb("crow", [P, N_GROUP, BLK])
        smax = sb("smax", [P, N_GROUP, BLK])
        smax2 = sb("smax2", [P, N_GROUP - 1, BLK])
        den = sb("den", [P, N_GROUP - 1, BLK])
        pairs = sb("pairs", [P, 2, 2, BLK, 2])
        own, other = pairs[:, 0, :, :, :], pairs[:, 1, :, :, :]
        shift = sb("shift", [P, 2, 2, BLK])
        shift_exp = sb("shift_exp", [P, 2, 2, BLK])
        shares = sb("shares", [P, 2, 2, BLK])
        total = sb("total", [P, 2, BLK])
        inverse = sb("inverse", [P, 2, BLK])
        factor = sb("factor", [P, 2, BLK])
        bn6 = sb("bn6", [P, BLK, 6])
        mv = sb("mv", [P, BLK, 2])
        lnstd = sb("lnstd", [P, BLK])
        lnrs = sb("lnrs", [P, BLK])

        qk = [work[:, j, :] for j in range(6)]
        v_tok = [work[:, 6 + g, :].rearrange("p (b e) -> p b e", b=BLK) for g in range(N_GROUP)]
        probs = work[:, 9:13, :].rearrange("p a (n k) -> p (a n) k", k=P)
        probsT = work[:, 13:17, :].rearrange("p a (n k) -> p (a n) k", k=P)
        ret_s = work[:, 0:3, :].rearrange("p a n -> p (a n)")
        ret_q, ret_k, ret_y = work[:, 3, :], work[:, 4, :], work[:, 8, :]
        ret_g = [work[:, 5 + i, :] for i in range(2)]
        merged = [work[:, 9 + n, :] for n in range(KT)]
        gates = [work[:, 17 + n, :] for n in range(2)]
        sg_u = [work[:, n, :] for n in range(HEADS)]
        sg_v = work[:, 4:8, :]
        row_sq = [in_high[:, 8:10, :], in_low[:, 8:10, :]]
        ret_std, k_std2 = work[:, 16, :], work[:, 17, :]
        ssq = work[:, 12, :]
        RS_OFF = [m * SEQ - P * m * (m - 1) // 2 for m in range(BLK)]

        psum = [ctx.enter_context(nc.psum_tensor(f"bank{i}", [P, SEQ], F32)) for i in range(8)]
        main_bank, score_bank, turn_bank = psum[0:2], psum[2:4], psum[4:6]
        out_bank, stat_bank = psum[6], psum[7]

        raw_loaded = [signal(f"raw_loaded{r}", [(s, i) for s in range(r, SLABS, RAW_SLOTS) for i in range(16)])
                      for r in range(RAW_SLOTS)]
        split_ahead = [(s,) for s in range(SPLIT_AHEAD)]
        part_high_w = signal("weight_high_ready", keys("split_high"), split_ahead)
        part_low_w = signal("weight_low_ready", keys("split_low"), split_ahead)
        tile_done = signal("slab_used_tile_done", PROJECTION_EVENTS)
        slab_used = Signal(tile_done.sem, PROJECTION_EVENTS)
        for i, bs in enumerate(BLOCKS):
            for s in {b[0] for b in bs}:
                if LAST_BLOCK[s] == (i, bs[-1]):
                    slab_used.number["slab", s] = tile_done.number[i,]
        tile_stored = signal("tile_stored", keys("evac"))
        activated = signal("activated", [k for k in keys("evac") if TILES[k[0]][0] in ACTIVATED_ROLES])
        squared = signal("squared", keys("square"), [("n", 0, n) for n in range(KT)])
        summed = signal("squares_summed", keys("sumsq"), [("n", 0, n) for n in range(1, KT)])
        stat_done = signal("stat_done", keys("stat"))
        rstd_kept = signal("norm_rstd_kept", keys("keep_rstd"))
        std_ready = signal("std_ready", keys("rstd"))
        sq_high_ready = signal("squares_high_ready", keys("split_sq"))
        sq_split = signal("squares_split", keys("split_sq"))
        rowstat_done = signal("rowstat_done", keys("rowstat"))
        rowstd_ready = signal("rowstd_ready", keys("rowstd"))
        rstd_ready = signal("rstd_ready", keys("rstd"))
        bcast_done = signal("bcast_done", keys("bcast"))
        product = signal("product_ready", PROD_KEYS)
        h_ahead = [("h", 0, n) for n in range(KT)]
        high_ready = signal("high_ready", keys("high"), h_ahead)
        low_ready = signal("low_ready", keys("low"), h_ahead)
        k_scaled = signal("k_scaled", keys("rowscale", "ck"))
        rotated = signal("rotated", keys("rotate"))
        v_turned = signal("v_turned", keys("vtrans"))
        v_stored = signal("v_stored", keys("vtrans"))
        scored = signal("scored", [u for u in S_USERS])
        score_taken = signal("score_taken", [u for u in S_USERS])
        max_ready = signal("max_ready", keys("expo"))
        exp_ready = signal("exp_ready", keys("expo"))
        pairs_ready = signal("pairs_ready", keys("gather"))
        shift_ready = signal("shift_ready", keys("weigh"))
        shift_exp_ready = signal("shift_exp_ready", keys("weigh"))
        probs_ready = signal("probs_ready", keys("weigh"))
        probs_turned = signal("probs_turned", keys("ptrans"))
        probsT_stored = signal("probsT_stored", keys("ptrans"))
        pv_done = signal("pv_done", keys("pv"))
        ret_done = signal("ret_done", keys("rpv"))
        ret_copied = signal("ret_copied", keys("ocopy"))
        ln_var = signal("ln_var_ready", [()])
        ln_std = signal("ln_std_ready", [()])
        sqrt_loaded = signal("sqrt_loaded", [(i,) for i in range(len(keys("load_sqrt")))])
        ln_done = signal("ln_done", keys("ln"))
        vector_chain = ctx.enter_context(nc.semaphore("vector_chain"))
        ident_loaded = ctx.enter_context(nc.semaphore("ident_loaded"))
        first_gain_loaded = ctx.enter_context(nc.semaphore("first_gain_loaded"))
        tables_loaded = ctx.enter_context(nc.semaphore("tables_loaded"))
        consts_set = ctx.enter_context(nc.semaphore("consts_set"))
        vec_loaded = ctx.enter_context(nc.semaphore("vec_loaded"))
        spatial_loaded = ctx.enter_context(nc.semaphore("spatial_loaded"))
        pairs_written = ctx.enter_context(nc.semaphore("pairs_written"))
        pairs_swapped = ctx.enter_context(nc.semaphore("pairs_swapped"))
        decay_loaded = ctx.enter_context(nc.semaphore("decay_loaded"))
        wait_carried = ctx.enter_context(nc.semaphore("wait_carried"))
        out_stored = ctx.enter_context(nc.semaphore("out_stored"))
        x_loaded = [ctx.enter_context(nc.semaphore(f"x_loaded{n}")) for n in range(KT)]

        def layer_base(eng, layer):
            base = eng.snap(layer * STRIDE)
            eng.get_value_cache().nocache = True
            return base

        def by_phase(dst, src, other, permuted):
            if not permuted:
                return dst, src, other
            return (dst.rearrange("p (r i) -> p i r", r=PHASES), src.rearrange("p (i r) -> p i r", r=PHASES),
                    other.rearrange("p (i r) -> p i r", r=PHASES))

        def own_wait(eng):
            eng.sem_inc(wait_carried, 1)

        def wait_square_read(eng, base, key):
            n = SQ_KEYS.index(key)
            before = SQ_KEYS[n - 2] if n >= 2 else ("n", 0, KT - 2 + n)
            if before in ROW_KEYS:
                eng.wait_ge(sq_split.sem, sq_split.at(base, *before))
            elif before[0] == "n":
                eng.wait_ge(summed.sem, summed.at(base, "n", before[1], max(before[2], 1)))
            else:
                eng.wait_ge(stat_done.sem, stat_done.at(base, *before))

        def square_parts(key):
            return [part[:, ROW_KEYS.index(key) % 2, :] for part in row_sq]

        def std_place(key):
            if key[0] == "r":
                return ret_std
            return prod[:, key[2], :] if key[2] < 2 else k_std2

        def wait_turn_bank(pe, base, n):
            if n < 2:
                return
            u = T_USERS[n - 2]
            if u[0] == "vtrans":
                pe.wait_ge(v_stored.sem, v_stored.at(base, *u[1:]))
            elif u[0] == "ptrans":
                pe.wait_ge(probsT_stored.sem, probsT_stored.at(base, *u[1:]))
            elif u[0] == "rowstat":
                pe.wait_ge(rowstd_ready.sem, rowstd_ready.at(base, *u[1:]))
            else:
                pe.wait_ge(rstd_kept.sem, rstd_kept.at(base, u[2]))

        def fill_up(eng, sig):
            eng.sem_inc(sig.sem, STRIDE - sig.ahead - sig.count)

        def close(eng, base, sigs):
            for sig in sigs:
                eng.wait_ge(sig.sem, base + sig.ahead + sig.count)
                fill_up(eng, sig)

        def parts(key):
            kind = key[0]
            if kind == "h":
                return h_high[:, key[2], :], h_low[:, key[2], :]
            n = {"yc": 0, "ys": 0, "yr": 4, "m": 4, "f": 0}[kind] + key[-1]
            return in_high[:, n, :], in_low[:, n, :]

        def input_tile(i, k):
            t = TILES[i]
            key = {"proj": lambda: ({2: "yc", 0: "yr", 1: "ys"}[t[1]], k),
                   "wo": lambda: ("m", k), "down": lambda: ("f", t[1], k)}.get(
                t[0], lambda: ("h", 1 if t[0] in ("fgate", "fup") else 0, k))()
            return key, parts(key)

        def sum_squares(eng, base, w, n):
            eng.wait_ge(squared.sem, squared.at(base, "n", w, n))
            if n > 1:
                eng.wait_ge(summed.sem, summed.at(base, "n", w, n - 1))
            eng.tensor_tensor(ssq, sq[:, 0, :] if n == 1 else ssq, sq[:, n % 2, :], ALU.add).then_inc(summed.sem, 1)

        block = ctx.enter_context(nc.Block())

        @block.gpsimd
        def _(pool):
            for n in range(1, KT):
                sum_squares(pool, 0, 0, n)

        @block.sync
        def _(sp):
            def load(base, s, row_of):
                slot = s % RAW_SLOTS
                sp.dma_start(raw[:, slot, :, :].rearrange("p a n -> p (a n)"),
                             weights[bass.ds(row_of, 1)].rearrange("a p n -> (a p) n")).then_inc(
                    raw_loaded[slot].sem, 16)

            def load_vecs(layer):
                sp.dma_start(vec[:, :], vecs[bass.ds(layer, 1)].rearrange("a p n -> (a p) n")).then_inc(
                    vec_loaded, 16)

            def load_spatial(layer):
                sp.dma_start(sgw[:, :, :], spatial[bass.ds(layer, 1)].rearrange("a p g n -> (a p) g n")).then_inc(
                    spatial_loaded, 16)
                sp.dma_start(row[:, :, :].rearrange("p r n -> p (r n)"),
                             rows[bass.ds(layer, 1)].rearrange("a r n -> (a r n)").partition_broadcast(P)).then_inc(
                    spatial_loaded, 16)

            def load_decay(base, h):
                if h > 0:
                    sp.wait_ge(score_taken.sem, score_taken.at(base, "rscore", h - 1, BLK - 1))
                sp.dma_start(decay_sb[:, :], decay[h]).then_inc(decay_loaded, 16)

            def behind(tile):
                return max(b[0] for b in BLOCKS[AT[tile]]) + RAW_SLOTS

            order = {s: n for n, s in enumerate(STEPS)}

            def load_behind(*step):
                return next(s for s in range(RAW_SLOTS + SPLIT_AHEAD, SLABS)
                            if order["split_low", s - RAW_SLOTS] > order[step])

            swap_at = {load_behind("swap", h): h for h in range(HEADS)}

            def write_pairs(base, h):
                sp.wait_ge(pairs_ready.sem, pairs_ready.at(base, h))
                sp.dma_start(pairs_dram[h, 0].rearrange("(b p) q -> p b q", p=P), own[:, 0, :, :]).then_inc(
                    pairs_written, 16)
                sp.dma_start(pairs_dram[h, 1].rearrange("(p r) q -> p r q", r=PHASES), own[:, 1, :, :]).then_inc(
                    pairs_written, 16)

            def read_pairs(base, h):
                sp.wait_ge(pairs_written, base + 32 * (h + 1))
                sp.dma_start(other[:, 1, :, :], pairs_dram[h, 0].rearrange("(p r) q -> p r q", r=PHASES)).then_inc(
                    pairs_swapped, 16)
                sp.dma_start(other[:, 0, :, :], pairs_dram[h, 1].rearrange("(b p) q -> p b q", p=P)).then_inc(
                    pairs_swapped, 16)

            decay_at = {behind(("k", 1, 0)): 0} | {load_behind("rscore", h - 1, BLK - 1): h
                                                    for h in range(1, HEADS)}

            sp.dma_start(first_gain[:, :], gain_first).then_inc(first_gain_loaded, 16)
            for n in range(KT):
                sp.dma_start(xT[:, n, :], x_in[:, n, :]).then_inc(x_loaded[n], 16)
                if n == 1:
                    load(0, 0, 0)
            sp.dma_start(ident[:, :], ident_in).then_inc(ident_loaded, 16)
            for s in range(1, RAW_SLOTS):
                load(0, s, s)
            sp.dma_start(mask_bits[:, :, :], masks).then_inc(tables_loaded, 16)
            sp.dma_start(rot[:, :, :], rotation).then_inc(tables_loaded, 16)
            load_spatial(0)
            with sp.Fori(0, DEPTH) as layer:
                base = layer_base(sp, layer)
                sp.wait_ge(low_ready.sem, low_ready.at(base, "h", 0, KT - 1))
                load_vecs(layer)
                for s in range(RAW_SLOTS, SLABS + RAW_SLOTS):
                    slot = (s if s < SLABS else s - SLABS) % RAW_SLOTS
                    if s in swap_at:
                        write_pairs(base, swap_at[s])
                    if s - 1 in swap_at:
                        read_pairs(base, swap_at[s - 1])
                    before = s - RAW_SLOTS if s < SLABS else max(u for u in range(SLABS) if u % RAW_SLOTS == slot)
                    sp.wait_ge(part_low_w.sem, part_low_w.at(base, before))
                    if s >= SLABS:
                        fill_up(sp, raw_loaded[slot])
                    load(base, slot if s >= SLABS else s, layer * SLABS + s)
                    if s in decay_at:
                        load_decay(base, decay_at[s])
                    if s == behind(("proj", 1, 0)):
                        sp.wait_ge(score_taken.sem, score_taken.at(base, "mix", HEADS - 1))
                        sp.wait_ge(spatial_loaded, base + 32)
                        sp.sem_inc(spatial_loaded, STRIDE - 32)
                        load_spatial(layer + 1)
                for sem, count in ((vec_loaded, 16), (pairs_written, 32 * HEADS), (pairs_swapped, 32 * HEADS)):
                    sp.wait_ge(sem, base + count)
                    sp.sem_inc(sem, STRIDE - count)
                sp.wait_ge(decay_loaded, base + 16 * HEADS)
                sp.sem_inc(decay_loaded, STRIDE - 16 * HEADS)
            for n in range(KT):
                sp.wait_ge(tile_stored.sem, tile_stored.at((DEPTH - 1) * STRIDE, AT["down", 1, n]))
                sp.dma_start(out[:, n, :], xT[:, n, :]).then_inc(out_stored, 16)
            for s in range(RAW_SLOTS):
                sp.wait_ge(raw_loaded[s].sem, DEPTH * STRIDE + 16)
            sp.wait_ge(spatial_loaded, DEPTH * STRIDE + 32)
            sp.wait_ge(out_stored, 16 * KT)

        @block.tensor
        def _(pe):
            pe.wait_ge(consts_set, 4)

            def matmul(o, w, m, start, stop):
                return pe.matmul(o, w, m, start=start, stop=stop)

            seen_inputs = set()

            def main(base, i, first, end):
                if i >= 2 and first == 0:
                    pe.wait_ge(tile_stored.sem, tile_stored.at(base, i - 2))
                o, blocks = main_bank[i % 2], BLOCKS[i]
                for n in range(first, end):
                    s, place, k = blocks[n]
                    if FIRST_USE[s] == i and (n == 0 or blocks[n - 1][0] != s):
                        pe.wait_ge(part_low_w.sem, part_low_w.at(base, s))
                    key, (hi, lo) = input_tile(i, k)
                    if key not in seen_inputs:
                        seen_inputs.add(key)
                        pe.wait_ge(low_ready.sem, low_ready.at(base, *key))
                    wh, wl = w_high[:, PART_SLOT[s], place, :], w_low[:, PART_SLOT[s], place, :]
                    matmul(o[:, :], wh, hi, n == 0, False)
                    matmul(o[:, :], wh, lo, False, False)
                    last = matmul(o[:, :], wl, hi, False, n == len(blocks) - 1)
                    if n == len(blocks) - 1:
                        last.then_inc(tile_done.sem, 1)
                    elif LAST_BLOCK[s] == (i, (s, place, k)):
                        last.then_inc(slab_used.sem, 1)

            def stat(base, key):
                group = key[:2]
                if (key[0] == "n" or key[2] == 0) and STAT_GROUPS.index(group) > 0:
                    pe.wait_ge(std_ready.sem, std_ready.at(base, *STAT_GROUPS[STAT_GROUPS.index(group) - 1]))
                if key[0] == "n":
                    pe.wait_ge(summed.sem, summed.at(base, *key, KT - 1))
                    squares, col = ssq, 0
                else:
                    pe.wait_ge(squared.sem, squared.at(base, *key))
                    squares, col = sq[:, SQ_KEYS.index(key) % 2, :], BLK * key[2]
                for b in range(BLK):
                    last = matmul(stat_bank[:, col + b:col + b + 1], squares[:, b * P:(b + 1) * P], ones[:, 0:1],
                                  True, True)
                last.then_inc(stat_done.sem, 1)

            def turn(base, user):
                n = T_USERS.index(user)
                wait_turn_bank(pe, base, n)
                return turn_bank[n % 2]

            def score_target(base, user):
                n = S_USERS.index(user)
                if n >= 2:
                    pe.wait_ge(score_taken.sem, score_taken.at(base, *S_USERS[n - 2]))
                return score_bank[n % 2]

            with pe.Fori(0, DEPTH * STRIDE, STRIDE) as base:
                pe.get_value_cache().nocache = True
                for kind, *key in STEPS:
                    key = tuple(key)
                    if kind == "main":
                        main(base, *key)
                    elif kind == "stat":
                        stat(base, key)
                    elif kind == "bcast":
                        o = turn(base, (kind,) + key)
                        if key == ("n", 0):
                            pe.wait_ge(ident_loaded, 16)
                        pe.wait_ge(rstd_ready.sem, rstd_ready.at(base, *key))
                        for b in range(BLK):
                            last = pe.transpose(o[:, b * P:(b + 1) * P],
                                                rs[:, b:b + 1].broadcast_to([P, P]), ident[:, :])
                        last.then_inc(bcast_done.sem, 1)
                    elif kind == "rowstat":
                        o = turn(base, (kind,) + key)
                        pe.wait_ge(sq_split.sem, sq_split.at(base, *key))
                        high, low = square_parts(key)
                        matmul(o[:, :], ones_r[:, :], high, True, False)
                        matmul(o[:, :], ones_r[:, :], low, False, True).then_inc(rowstat_done.sem, 1)
                    elif kind == "vtrans":
                        o = turn(base, (kind,) + key)
                        ready = activated if key[0] == "sv" else tile_stored
                        pe.wait_ge(ready.sem, ready.at(base, AT[key]))
                        slot = SCALED_TILES.index(key) % 2
                        for b in range(BLK):
                            last = pe.transpose(o[:, b * P:(b + 1) * P], scaled[:, slot, b * P:(b + 1) * P],
                                                ident[:, :])
                        last.then_inc(v_turned.sem, 1)
                    elif kind == "scores":
                        h, u = key
                        o = score_target(base, (kind,) + key)
                        for g in sorted({r[0] for r in rows_of_unit(u)}):
                            pe.wait_ge(k_scaled.sem, k_scaled.at(base, "ck", h, g))
                        for g, b, first, n in rows_of_unit(u):
                            at, k0 = (first - UNITS[u][0]) * P, SCORE_BLOCKS[first][2]
                            last = matmul(o[:, at:at + n * P], qk[g][:, b * P:(b + 1) * P],
                                          qk[3 + g][:, k0 * P:(k0 + n) * P], True, True)
                        last.then_inc(scored.sem, 1)
                    elif kind == "ptrans":
                        h, u = key
                        pe.wait_ge(probs_ready.sem, probs_ready.at(base, h))
                        o = turn(base, (kind,) + key)
                        for j, n in enumerate(UNITS[u]):
                            last = pe.transpose(o[:, j * P:(j + 1) * P], probs[:, n, :], ident[:, :])
                        last.then_inc(probs_turned.sem, 1)
                    elif kind == "pv":
                        h, g = key
                        if g == 0 and h > 0:
                            pe.wait_ge(low_ready.sem, low_ready.at(base, "yc", h - 1))
                        pe.wait_ge(v_stored.sem, v_stored.at(base, "v", h, g))
                        pe.wait_ge(probsT_stored.sem, probsT_stored.at(base, h, UNIT_OF_GROUP[g][-1]))
                        for n, (of, b, kb) in enumerate(SCORE_BLOCKS):
                            if of == g:
                                o = (out_bank[:, b * P:(b + 1) * P] if g == 0 else
                                     out_bank[:, :].rearrange("p (i r) -> p r i", r=PHASES)[:, b, :])
                                last = matmul(o, v_tok[g][:, kb, :], probsT[:, n, :],
                                              n == 0, n == len(SCORE_BLOCKS) - 1)
                        last.then_inc(pv_done.sem, 1)
                    elif kind == "fill_ahead":
                        close(pe, base, [stat_done, rowstat_done, bcast_done, v_turned, scored, probs_turned, pv_done, ret_done])
                    elif kind == "rscore":
                        h, m = key
                        o = score_target(base, ("rscore", h, m))
                        pe.wait_ge(rotated.sem, rotated.at(base, "rk", h))
                        matmul(o[:, 0:SEQ - m * P], ret_k[:, m * P:(m + 1) * P], ret_q[:, m * P:SEQ],
                               True, True).then_inc(scored.sem, 1)
                    elif kind == "rpv":
                        h, = key
                        if h == 0:
                            pe.wait_ge(low_ready.sem, low_ready.at(base, "yc", HEADS - 1))
                        else:
                            pe.wait_ge(ret_copied.sem, ret_copied.at(base, h - 1))
                        pe.wait_ge(v_stored.sem, v_stored.at(base, "rv", h))
                        for m in range(BLK):
                            pe.wait_ge(score_taken.sem, score_taken.at(base, "rscore", h, m))
                            last = matmul(out_bank[:, m * P:SEQ], ret_v[:, m, :], ret_s[:, RS_OFF[m]:RS_OFF[m] + SEQ - m * P],
                                          m == 0, m == BLK - 1)
                        last.then_inc(ret_done.sem, 1)
                    elif kind == "mix":
                        g, = key
                        o = score_target(base, ("mix", g))
                        pe.wait_ge(ln_done.sem, ln_done.at(base, BLK - 1))
                        for b in range(BLK):
                            last = matmul(o[:, b * P:(b + 1) * P], sg_v[:, b, g * P:(g + 1) * P], sgw[:, g, :],
                                          True, True)
                        last.then_inc(scored.sem, 1)
                close(pe, base, [tile_done])

        @block.scalar
        def _(act):
            act.wait_ge(consts_set, 4)

            def split(base, *key):
                s = key[-1]
                raw_base = base + STRIDE if "next" in key else base
                act.wait_ge(raw_loaded[s % RAW_SLOTS].sem, raw_base + 16 * (s // RAW_SLOTS + 1))
                if "next" in key or s >= SPLIT_AHEAD:
                    if "next" in key or s >= PART_SLOTS:
                        act.wait_ge(slab_used.sem, slab_used.at(base, "slab", SLOT_BEFORE[s]))
                act.activation(w_high[:, PART_SLOT[s], :, :], raw[:, s % RAW_SLOTS, :, :], ACT.Copy).then_inc(
                    part_high_w.sem, 1)

            def high_of_x(dst, n, gain):
                act.activation(dst, xT[:, n, :], ACT.Copy, scale=gain[:, n:n + 1]).then_inc(high_ready.sem, 1)

            act.activation(sqrt_out[:, :], eps[:, :], ACT.Sqrt)
            act.wait_ge(first_gain_loaded, 16)
            for n in range(KT):
                act.wait_ge(x_loaded[n], 16)
                high_of_x(h_high[:, n, :], n, first_gain)
                if n >= 2:
                    act.wait_ge(summed.sem, summed.at(0, "n", 0, max(n - 2, 1)))
                act.activation(sq[:, n % 2, :], xT[:, n, :], ACT.Square).then_inc(squared.sem, 1)
                if n == 1:
                    split(0, 0)
            for s in range(1, SPLIT_AHEAD):
                split(0, s)
            with act.Fori(0, DEPTH * STRIDE, STRIDE) as base:
                act.get_value_cache().nocache = True
                for kind, *key in STEPS:
                    key = tuple(key)
                    if kind == "split_high":
                        split(base, *key)
                    elif kind == "fill_ahead":
                        close(act, base, [squared, sq_high_ready, rowstd_ready, high_ready, activated, std_ready, v_stored, exp_ready,
                                          shift_exp_ready, probsT_stored, ret_copied, ln_std])
                    elif kind == "fill_split":
                        close(act, base, [part_high_w])
                    elif kind == "load_sqrt":
                        act.activation(sqrt_out[:, :], eps[:, :], ACT.Sqrt).then_inc(sqrt_loaded.sem, 1)
                    elif kind == "evac":
                        i, = key
                        t = TILES[i]
                        if t[0] not in ACTIVATED_ROLES:
                            continue
                        act.wait_ge(tile_stored.sem, tile_stored.at(base, i))
                        src = scaled[:, SCALED_TILES.index(t) % 2, :]
                        if t[0] == "sv":
                            dst, func = src, ACT.Gelu_apprx_tanh
                        elif t[0] == "rg":
                            if t[1] > 1:
                                act.wait_ge(product.sem, product.at(base, "yr", t[1] - 2))
                            dst, func = ret_g[t[1] % 2], ACT.Silu
                        elif t[0] == "su":
                            dst, func = sg_u[t[1]], ACT.Gelu_apprx_tanh
                        else:
                            n = GATE_TILES.index(i)
                            dst, func = gates[n % 2], ACT.Sigmoid if t[0] == "gate" else ACT.Silu
                            if n >= 2:
                                u = TILES[GATE_TILES[n - 2]]
                                j = AT["proj" if u[0] == "gate" else "fup", u[1], u[2]]
                                act.wait_ge(tile_stored.sem, tile_stored.at(base, j))
                        act.activation(dst, src, func).then_inc(activated.sem, 1)
                    elif kind == "square":
                        wait_square_read(act, base, key)
                        if key[0] == "n":
                            src = xT[:, key[2], :]
                        elif key[0] == "r":
                            src = ret_y[:, :]
                            act.wait_ge(ret_copied.sem, ret_copied.at(base, key[1]))
                        else:
                            src = qk[key[2] + (3 if key[0] == "ck" else 0)]
                            act.wait_ge(tile_stored.sem, tile_stored.at(base, AT[key[0][1], key[1], key[2]]))
                        act.activation(sq[:, SQ_KEYS.index(key) % 2, :], src, ACT.Square).then_inc(squared.sem, 1)
                    elif kind == "split_sq":
                        n = ROW_KEYS.index(key)
                        if n >= 2:
                            act.wait_ge(rowstat_done.sem, rowstat_done.at(base, *ROW_KEYS[n - 2]))
                        src = ret_y if key[0] == "r" else qk[3 + key[2]]
                        act.activation(square_parts(key)[0], src, ACT.Square).then_inc(sq_high_ready.sem, 1)
                    elif kind == "rowstd":
                        act.wait_ge(rowstat_done.sem, rowstat_done.at(base, *key))
                        if key[1] > 0:
                            if key[0] == "r":
                                act.wait_ge(product.sem, product.at(base, "yr", key[1] - 1))
                            else:
                                act.wait_ge(k_scaled.sem, k_scaled.at(base, "ck", key[1] - 1, key[2]))
                        act.activation(std_place(key), turn_bank[T_USERS.index(("rowstat",) + key) % 2][:, :], ACT.Sqrt,
                                       bias=eps[:, 0:1], scale=1.0 / P).then_inc(rowstd_ready.sem, 1)
                    elif kind == "rstd":
                        n = STAT_GROUPS.index(key)
                        if n > 0:
                            act.wait_ge(rstd_ready.sem, rstd_ready.at(base, *STAT_GROUPS[n - 1]))
                        act.wait_ge(stat_done.sem, stat_done.at(base, *([k for k in keys("stat") if k[:2] == key][-1])))
                        cols = N_GROUP * BLK if key[0] == "cq" else BLK
                        width = D_MODEL if key[0] == "n" else P
                        src = stat_bank[:, 0:cols]
                        act.activation(std[:, 0:cols], src, ACT.Sqrt, bias=(eps_q if key[0] == "cq" else eps)[:, 0:1],
                                       scale=1.0 if key[0] == "cq" else 1.0 / width).then_inc(std_ready.sem, 1)
                    elif kind == "high":
                        if key[0] == "h":
                            tile = AT["wo", key[2]] if key[1] == 1 else AT["down", 1, key[2]]
                            act.wait_ge(tile_stored.sem, tile_stored.at(base, tile))
                            high_of_x(parts(key)[0], key[2], vec[:, 0:KT] if key[1] == 1 else vec[:, KT:2 * KT])
                            continue
                        if key[0] == "yc":
                            act.wait_ge(pv_done.sem, pv_done.at(base, key[1], N_GROUP - 1))
                            src = out_bank[:, :]
                        else:
                            act.wait_ge(product.sem, product.at(base, *key))
                            src = prod[:, PROD_KEYS.index(key) % 2, :]
                        act.activation(parts(key)[0], src, ACT.Copy).then_inc(high_ready.sem, 1)
                    elif kind == "vtrans":
                        act.wait_ge(v_turned.sem, v_turned.at(base, *key))
                        src = turn_bank[T_USERS.index((kind,) + key) % 2][:, :].rearrange("p (b e) -> p b e", b=BLK)
                        if key[0] == "v":
                            dst = v_tok[key[2]]
                        elif key[0] == "rv":
                            dst = ret_v[:, :, :]
                        else:
                            dst = sg_v[:, :, key[1] * P:(key[1] + 1) * P]
                        act.activation(dst, src, ACT.Copy).then_inc(v_stored.sem, 1)
                    elif kind == "expo":
                        h, step = key
                        act.wait_ge(max_ready.sem, max_ready.at(base, h, step))
                        for u in ((0, 1), (2, 3))[step]:
                            for g, b, first, n in rows_of_unit(u):
                                p = probs[:, first:first + n, :]
                                e = act.activation(p, p, ACT.Exp, bias=own[:, step, b, 0:1], scale=crow[:, g, b:b + 1],
                                                   accum_out=own[:, 0, b, 1:2] if g == 0 else den[:, g - 1, b:b + 1])
                        e.then_inc(exp_ready.sem, 1)
                    elif kind == "weigh":
                        act.wait_ge(shift_ready.sem, shift_ready.at(base, *key))
                        act.activation(shift_exp[:, :, :, :], shift[:, :, :, :], ACT.Exp).then_inc(shift_exp_ready.sem, 1)
                    elif kind == "ptrans":
                        h, u = key
                        act.wait_ge(probs_turned.sem, probs_turned.at(base, h, u))
                        n = len(UNITS[u])
                        src = turn_bank[T_USERS.index((kind,) + key) % 2][:, 0:n * P].rearrange("p (n k) -> p n k", k=P)
                        act.activation(probsT[:, UNITS[u][0]:UNITS[u][0] + n, :], src, ACT.Copy).then_inc(
                            probsT_stored.sem, 1)
                    elif kind == "ocopy":
                        h, = key
                        act.wait_ge(ret_done.sem, ret_done.at(base, h))
                        if h > 0:
                            act.wait_ge(product.sem, product.at(base, "yr", h - 1))
                        act.activation(ret_y[:, :], out_bank[:, :], ACT.Copy).then_inc(ret_copied.sem, 1)
                    elif kind == "lnvar":
                        act.wait_ge(ln_var.sem, ln_var.at(base))
                        act.activation(lnstd[:, :], mv[:, :, 1], ACT.Sqrt, bias=eps[:, 0:1]).then_inc(ln_std.sem, 1)
                close(act, base, [sqrt_loaded])

        @block.vector
        def _(dve):
            dve.memset(ones[:, :], 1.0).then_inc(consts_set, 1)
            dve.wait_ge(consts_set, 1)
            dve.tensor_copy(ones_r[:, :], ones[:, :]).then_inc(consts_set, 1)
            dve.memset(eps[:, :], EPS).then_inc(consts_set, 1)
            dve.memset(eps_q[:, :], EPS * P).then_inc(consts_set, 1)
            def split(base, *key):
                s = key[-1]
                dve.wait_ge(part_high_w.sem, part_high_w.at(base, *key))
                dve.tensor_tensor(w_low[:, PART_SLOT[s], :, :], raw[:, s % RAW_SLOTS, :, :],
                                  w_high[:, PART_SLOT[s], :, :], ALU.subtract).then_inc(part_low_w.sem, 1)

            def low_of_x(dst, high, n, gain):
                dve.scalar_tensor_tensor(dst, xT[:, n, :], gain[:, n:n + 1], high, ALU.mult, ALU.subtract).then_inc(
                    low_ready.sem, 1)

            dve.wait_ge(first_gain_loaded, 16)
            for n in range(KT):
                dve.wait_ge(high_ready.sem, high_ready.at(0, "h", 0, n))
                low_of_x(h_low[:, n, :], h_high[:, n, :], n, first_gain)
                if n == 1:
                    split(0, 0)
            for s in range(1, SPLIT_AHEAD):
                split(0, s)
            with dve.Fori(0, DEPTH * STRIDE, STRIDE) as base:
                dve.get_value_cache().nocache = True
                chained = [0]

                def chain(ins):
                    ins.then_inc(vector_chain, 1)
                    chained[0] += 1
                    dve.wait_ge(vector_chain, base + chained[0])

                def product_slot(key):
                    n = PROD_KEYS.index(key)
                    if n >= 2:
                        dve.wait_ge(low_ready.sem, low_ready.at(base, *PROD_KEYS[n - 2]))
                    return prod[:, n % 2, :]

                tmp_read = []

                def tmp_free():
                    if tmp_read:
                        sig, key = tmp_read[-1]
                        dve.wait_ge(sig.sem, sig.at(base, *key))

                for kind, *key in STEPS:
                    key = tuple(key)
                    if kind == "split_low":
                        split(base, *key)
                    elif kind == "fill_split":
                        close(dve, base, [part_low_w])
                    elif kind == "fill_ahead":
                        close(dve, base, [summed, sq_split, low_ready, rstd_kept, rstd_ready, product, rotated, k_scaled,
                                          score_taken, max_ready, pairs_ready, shift_ready, probs_ready, ln_var,
                                          ln_done])
                        dve.wait_ge(vector_chain, base + chained[0])
                        dve.sem_inc(vector_chain, STRIDE - chained[0])
                        chained_before = chained[0]
                    elif kind == "sumsq":
                        sum_squares(dve, base, *key[1:])
                    elif kind == "keep_rstd":
                        w, = key
                        dve.wait_ge(bcast_done.sem, bcast_done.at(base, "n", w))
                        dve.tensor_copy(norm_rstd[:, :], turn_bank[T_USERS.index(("bcast", "n", w)) % 2][:, :]).then_inc(
                            rstd_kept.sem, 1)
                        dve.wait_ge(rstd_kept.sem, rstd_kept.at(base, w))
                        if w == 0:
                            dve.wait_ge(vec_loaded, base + 16)
                            chain(dve.tensor_tensor(gqk[:, :], vec[:, 20:21], vec[:, 21:22], ALU.mult))
                    elif kind == "evac":
                        i, = key
                        t = TILES[i]
                        dve.wait_ge(tile_done.sem, tile_done.at(base, i))
                        src = main_bank[i % 2][:, :]
                        if t[0] in SCALED_ROLES:
                            n = SCALED_TILES.index(t)
                            if n >= 2:
                                u = SCALED_TILES[n - 2]
                                if u[0] in ("rq", "rk"):
                                    dve.wait_ge(rotated.sem, rotated.at(base, *u))
                                elif u[0] in ("v", "rv", "sv"):
                                    dve.wait_ge(v_turned.sem, v_turned.at(base, *u))
                                else:
                                    dve.wait_ge(activated.sem, activated.at(base, AT[u]))
                            operands = by_phase(scaled[:, n % 2, :], src, norm_rstd[:, :], t[0] == "v" and t[2] > 0)
                            dve.tensor_tensor(*operands, ALU.mult).then_inc(tile_stored.sem, 1)
                        elif t[0] in ("q", "k"):
                            operands = by_phase(qk[t[2] + (3 if t[0] == "k" else 0)], src, norm_rstd[:, :], t[2] > 0)
                            dve.tensor_tensor(*operands, ALU.mult).then_inc(tile_stored.sem, 1)
                        elif t[0] == "proj":
                            _, br, n = t
                            dve.wait_ge(activated.sem, activated.at(base, AT["gate", br, n]))
                            g = gates[GATE_TILES.index(AT["gate", br, n]) % 2]
                            if br == 2:
                                dve.tensor_tensor(merged[n], src, g, ALU.mult).then_inc(tile_stored.sem, 1)
                            else:
                                tmp_free()
                                chain(dve.tensor_tensor(tmp[:, :], src, g, ALU.mult))
                                tmp_read.append((tile_stored, (i,)))
                                if br == 0:
                                    dve.tensor_tensor(merged[n], merged[n], tmp[:, :], ALU.add).then_inc(tile_stored.sem, 1)
                                else:
                                    dst = product_slot(("m", n))
                                    chain(dve.tensor_tensor(dst, merged[n], tmp[:, :], ALU.add))
                                    dve.sem_inc(product.sem, 1)
                                    dve.sem_inc(tile_stored.sem, 1)
                        elif t[0] in ("wo", "down"):
                            dve.tensor_tensor(xT[:, t[-1], :], src, xT[:, t[-1], :], ALU.add).then_inc(tile_stored.sem, 1)
                        else:
                            g = AT["fgate", t[1], t[2]]
                            dve.wait_ge(activated.sem, activated.at(base, g))
                            dst = product_slot(("f", t[1], t[2]))
                            tmp_free()
                            tmp_read.append((tile_stored, (i,)))
                            chain(dve.tensor_tensor(tmp[:, :], src, norm_rstd[:, :], ALU.mult))
                            chain(dve.tensor_tensor(dst, tmp[:, :], gates[GATE_TILES.index(g) % 2], ALU.mult))
                            dve.sem_inc(product.sem, 1)
                            dve.sem_inc(tile_stored.sem, 1)
                    elif kind == "rotate":
                        dst, half = ret_q if key[0] == "rq" else ret_k, P // 2
                        src = scaled[:, SCALED_TILES.index(key) % 2, :]
                        dve.wait_ge(tile_stored.sem, tile_stored.at(base, AT[key]))
                        tmp_free()
                        dve.tensor_tensor(dst, src, rot[:, 0, :], ALU.mult)
                        dve.tensor_tensor(tmp[0:half, :], src[half:P, :], rot[half:P, 1, :], ALU.mult)
                        chain(dve.tensor_tensor(tmp[half:P, :], src[0:half, :], rot[0:half, 1, :], ALU.mult))
                        dve.tensor_tensor(dst, dst, tmp[:, :], ALU.add).then_inc(rotated.sem, 1)
                        tmp_read.append((rotated, key))
                    elif kind == "low":
                        dve.wait_ge(high_ready.sem, high_ready.at(base, *key))
                        hi, lo = parts(key)
                        if key[0] == "h":
                            low_of_x(lo, hi, key[2], vec[:, 0:KT] if key[1] == 1 else vec[:, KT:2 * KT])
                            continue
                        src = out_bank[:, :] if key[0] == "yc" else prod[:, PROD_KEYS.index(key) % 2, :]
                        dve.tensor_tensor(lo, src, hi, ALU.subtract).then_inc(low_ready.sem, 1)
                    elif kind == "rstd":
                        dve.wait_ge(std_ready.sem, std_ready.at(base, *key))
                        if key[0] == "cq":
                            if key[1] > 0:
                                dve.wait_ge(exp_ready.sem, exp_ready.at(base, key[1] - 1, 1))
                            dve.reciprocal(crow[:, :, :].rearrange("p g b -> p (g b)"), std[:, :]).then_inc(
                                rstd_ready.sem, 1)
                        else:
                            if key[1] == 1:
                                dve.wait_ge(bcast_done.sem, bcast_done.at(base, "n", 0))
                            dve.reciprocal(rs[:, :], std[:, 0:BLK]).then_inc(rstd_ready.sem, 1)
                    elif kind == "split_sq":
                        dve.wait_ge(sq_high_ready.sem, sq_high_ready.at(base, *key))
                        high, low = square_parts(key)
                        dve.tensor_tensor(low, sq[:, SQ_KEYS.index(key) % 2, :], high, ALU.subtract).then_inc(
                            sq_split.sem, 1)
                    elif kind == "rowinv":
                        dve.wait_ge(rowstd_ready.sem, rowstd_ready.at(base, *key))
                        chain(dve.reciprocal(std_place(key), std_place(key)))
                    elif kind == "rowscale" and key[0] == "ck":
                        k = qk[3 + key[2]]
                        dve.scalar_tensor_tensor(k, k, gqk[:, 0:1], std_place(key), ALU.mult, ALU.mult).then_inc(
                            k_scaled.sem, 1)
                    elif kind == "rowscale":
                        h = key[1]
                        dve.wait_ge(activated.sem, activated.at(base, AT["rg", h]))
                        dst = product_slot(("yr", h))
                        tmp_free()
                        tmp_read.append((product, ("yr", h)))
                        chain(dve.scalar_tensor_tensor(tmp[:, :], ret_y[:, :], vec[:, 16 + h:17 + h], ret_std,
                                                       ALU.mult, ALU.mult))
                        dve.tensor_tensor(dst, tmp[:, :], ret_g[h % 2], ALU.mult).then_inc(product.sem, 1)
                    elif kind == "scores":
                        h, u = key
                        if key == (0, 0):
                            dve.wait_ge(tables_loaded, 32)
                        dve.wait_ge(scored.sem, scored.at(base, "scores", h, u))
                        own_wait(dve)
                        src = score_bank[S_USERS.index((kind,) + key) % 2]
                        for g, b, first, n in rows_of_unit(u):
                            at, m = (first - UNITS[u][0]) * P, mask_of(g, n)
                            last = dve.tensor_tensor_reduce(
                                probs[:, first:first + n, :].rearrange("p n k -> p (n k)"), src[:, at:at + n * P],
                                mask[:, m:m + n, :].rearrange("p a n -> p (a n)"), 1.0, -3e38,
                                ALU.add, ALU.max, smax[:, g, b:b + 1])
                        last.then_inc(score_taken.sem, 1)
                    elif kind == "expo":
                        h, step = key
                        dve.wait_ge(score_taken.sem, score_taken.at(base, "scores", h, 2 * step + 1))
                        dve.wait_ge(rstd_ready.sem, rstd_ready.at(base, "cq", h))
                        if step == 0:
                            dve.scalar_tensor_tensor(own[:, 0, :, 0], smax[:, 0, :], -1.0, crow[:, 0, :], ALU.mult,
                                                     ALU.mult).then_inc(max_ready.sem, 1)
                        else:
                            chain(dve.tensor_tensor(smax2[:, :, :], smax[:, 1:, :], crow[:, 1:, :], ALU.mult))
                            dve.tensor_reduce(own[:, 1, :, 0], smax2[:, :, :].rearrange("p g b -> p b g"), AX_X,
                                              ALU.max, negate=True).then_inc(max_ready.sem, 1)
                    elif kind == "gather":
                        h, = key
                        dve.wait_ge(exp_ready.sem, exp_ready.at(base, h, 1))
                        dve.tensor_tensor(own[:, 1, :, 1], den[:, 0, :], den[:, 1, :], ALU.add).then_inc(pairs_ready.sem, 1)
                    elif kind == "weigh":
                        h, = key
                        dve.wait_ge(pairs_swapped, base + 32 * (h + 1))
                        dve.tensor_tensor(shift[:, 0, :, :], other[:, :, :, 0], own[:, :, :, 0], ALU.subtract)
                        chain(dve.tensor_tensor(shift[:, 1, :, :], own[:, :, :, 0], other[:, :, :, 0], ALU.subtract))
                        dve.tensor_scalar(shift[:, :, :, :], shift[:, :, :, :], 0.0, None, ALU.min).then_inc(
                            shift_ready.sem, 1)
                        dve.wait_ge(shift_exp_ready.sem, shift_exp_ready.at(base, h))
                        chain(dve.tensor_tensor(shares[:, :, :, :], shift_exp[:, :, :, :], pairs[:, :, :, :, 1], ALU.mult))
                        chain(dve.tensor_tensor(total[:, :, :], shares[:, 0, :, :], shares[:, 1, :, :], ALU.add))
                        chain(dve.reciprocal(inverse[:, :, :], total[:, :, :]))
                        chain(dve.tensor_tensor(factor[:, :, :], inverse[:, :, :], shift_exp[:, 0, :, :], ALU.mult))
                        first = probs[:, 0, :]
                        dve.tensor_scalar(first, first, factor[:, 0, 0:1], None, ALU.mult)
                        p = probs[:, 1:7, :].rearrange("p (b k) n -> p b (k n)", k=2)
                        dve.tensor_tensor(p, p, factor[:, 0, 1:BLK].unsqueeze(2).broadcast_to([P, BLK - 1, 2 * P]), ALU.mult)
                        for g in range(1, N_GROUP):
                            at = SCORE_BLOCKS.index((g, 0, 0))
                            p = probs[:, at:at + PHASES, :]
                            last = dve.tensor_tensor(p, p, factor[:, 1, :].unsqueeze(2).broadcast_to([P, PHASES, P]),
                                                     ALU.mult)
                        last.then_inc(probs_ready.sem, 1)
                    elif kind == "rscore":
                        h, m = key
                        n = SEQ - m * P
                        dve.wait_ge(scored.sem, scored.at(base, "rscore", h, m))
                        dve.wait_ge(decay_loaded, base + 16 * (h + 1))
                        dve.tensor_tensor(ret_s[:, RS_OFF[m]:RS_OFF[m] + n],
                                          score_bank[S_USERS.index(("rscore", h, m)) % 2][:, 0:n],
                                          decay_sb[:, 0:n], ALU.mult).then_inc(score_taken.sem, 1)
                    elif kind == "lnvar":
                        dve.wait_ge(spatial_loaded, base + 32)
                        chain(dve.tensor_tensor(sgw[:, :, :], sgw[:, :, :],
                                                mask[:, SPATIAL_MASK:SPATIAL_MASK + 1, :].broadcast_to([P, HEADS, P]), ALU.mult))
                        for c in range(HEADS):
                            dve.wait_ge(v_stored.sem, v_stored.at(base, "sv", c))
                        for b in range(BLK):
                            last = dve.bn_stats(bn6[:, b, :], sg_v[:, b, :])
                        chain(last)
                        own_wait(dve)
                        for b in range(BLK):
                            last = dve.bn_aggr(mv[:, b, :], bn6[:, b, :])
                        last.then_inc(ln_var.sem, 1)
                    elif kind == "ln":
                        step, = key
                        if step == 0:
                            dve.wait_ge(ln_std.sem, ln_std.at(base))
                            chain(dve.reciprocal(lnrs[:, :], lnstd[:, :]))
                        v = sg_v[:, step, :]
                        chain(dve.tensor_scalar(v, v, mv[:, step, 0:1], lnrs[:, step:step + 1],
                                                ALU.subtract, ALU.mult))
                        chain(dve.tensor_tensor(v, v, row[:, 0, :], ALU.mult))
                        dve.tensor_tensor(v, v, row[:, 1, :], ALU.add).then_inc(ln_done.sem, 1)
                    elif kind == "mix":
                        g, = key
                        dve.wait_ge(scored.sem, scored.at(base, "mix", g))
                        dve.wait_ge(activated.sem, activated.at(base, AT["su", g]))
                        dst = product_slot(("ys", g))
                        src = score_bank[S_USERS.index(("mix", g)) % 2][:, :].rearrange("p (b n) -> p b n", b=BLK)
                        tmp_free()
                        tmp_read.append((product, ("ys", g)))
                        ins = dve.tensor_tensor(tmp[:, :].rearrange("p (b n) -> p b n", b=BLK), src,
                                                row[:, 2:3, g * P:(g + 1) * P].broadcast_to([P, BLK, P]), ALU.add)
                        ins.then_inc(score_taken.sem, 1)
                        dve.wait_ge(score_taken.sem, score_taken.at(base, "mix", g))
                        dve.tensor_tensor(dst, tmp[:, :], sg_u[g], ALU.mult).then_inc(product.sem, 1)
                assert chained[0] == chained_before
                close(dve, base, [tile_stored])



def _columns():
    ka, va, ga, ub, vb = 512, 1024, 1536, 2048, 2560
    qc = 3072
    kc, vc, gates = qc + 1536, qc + 3072, qc + 4608

    def of(t):
        if t[0] in "qkv":
            return {"q": qc, "k": kc, "v": vc}[t[0]] + t[2] * 512 + t[1] * P
        if t[0] == "gate":
            return gates + t[1] * D_MODEL + t[2] * P
        return {"rq": 0, "rk": ka, "rv": va, "rg": ga, "su": ub, "sv": vb}[t[0]] + t[1] * P
    return of


def _weights(w_in, w_branch, w_o, w_gate_up, w_down):
    of = _columns()
    out = np.empty((DEPTH * SLABS + RAW_SLOTS, P, 8, P), np.float32)
    for layer in range(DEPTH):
        for t, blocks in zip(TILES, BLOCKS):
            if t[0] == "proj":
                src, col, row0 = w_branch[layer, t[1]], t[2] * P, 0
            elif t[0] == "wo":
                src, col, row0 = w_o[layer], t[1] * P, 0
            elif t[0] in ("fgate", "fup"):
                src, col, row0 = w_gate_up[layer], (D_FF if t[0] == "fup" else 0) + (t[1] * FF_HALF + t[2]) * P, 0
            elif t[0] == "down":
                src, col, row0 = w_down[layer], t[2] * P, t[1] * FF_HALF * P
            else:
                src, col, row0 = w_in[layer], of(t), 0
            for s, place, k in blocks:
                r = row0 + k * P
                out[layer * SLABS + s, :, place, :] = src[r:r + P, col:col + P]
    out[DEPTH * SLABS:] = out[:RAW_SLOTS]
    return out.reshape(-1, P, 8 * P)


def _constants():
    f = np.float32
    half = P // 2
    inv = (f(1.0) / (f(ROPE_BASE) ** (np.arange(half, dtype=f) / f(half)))).astype(f)
    ang = (np.arange(SEQ, dtype=f)[:, None] * inv[None, :]).astype(f)
    cos, sin = np.cos(ang).T.astype(f), np.sin(ang).T.astype(f)
    rotation = np.stack([np.concatenate([cos, cos]), np.concatenate([sin, -sin])], axis=1)
    log_g = np.log1p(-(2.0 ** (-5.0 - np.arange(HEADS))))
    dist = np.arange(SEQ)[None, :] - np.arange(P)[:, None]
    decay = np.where(dist[None] >= 0, np.exp(log_g[:, None, None] * np.maximum(dist, 0)) * SCALE, 0.0).astype(f)
    q, k = np.arange(P)[:, None], np.arange(P)[None, :]
    causal = k <= q
    blocks = [(q + P - k) <= DILATIONS[0][0], causal] + [causal & ((q - k) % (d // PHASES) == 0) for _, d in DILATIONS[2:]]
    masks = [np.where(b, 0.0, NEG) for b in blocks] + [np.where(q <= k, 1.0, 0.0)]
    masks = (np.stack(masks, axis=1).astype(f).view(np.uint32) >> 16).astype(np.uint16)
    return rotation.astype(f), decay, masks, np.eye(P, dtype=f)


def kernel(x, g_mix, w_in, ret_norm_g, sg_ln_g, sg_ln_b, sg_w, sg_b, dil_q_norm_g, dil_k_norm_g, w_branch, w_o,
           g_ffn, w_gate_up, w_down):
    import concourse.bacc as bacc
    from concourse.bass_utils import run_bass_kernel_spmd

    def per_layer(a, n):
        return np.asarray(a).reshape(DEPTH, n, P).transpose(0, 2, 1)

    def and_again(a):
        return np.ascontiguousarray(np.concatenate([a, a[-1:]]))

    rotation, decay, masks, ident = _constants()
    arrays = {
        "x_t": np.ascontiguousarray(np.asarray(x)[0].T.reshape(KT, P, SEQ).transpose(1, 0, 2)),
        "weights": _weights(*(np.asarray(a) for a in (w_in, w_branch, w_o, w_gate_up, w_down))),
        "gain_of_first": np.ascontiguousarray(per_layer(g_mix, KT)[0]),
        "vecs": and_again(np.concatenate([per_layer(g_ffn, KT), and_again(per_layer(g_mix, KT))[1:],
                                          per_layer(ret_norm_g, HEADS),
                                          per_layer(dil_q_norm_g, 1), per_layer(dil_k_norm_g, 1)], axis=2)),
        "spatial": and_again(np.asarray(sg_w).transpose(0, 3, 1, 2)),
        "rows": and_again(np.stack([np.asarray(sg_ln_g), np.asarray(sg_ln_b), np.asarray(sg_b).reshape(DEPTH, -1)],
                                   axis=1)),
        "rotation": rotation, "decay": decay, "masks": masks, "ident": ident,
    }
    nc = bacc.Bacc("TRN2", target_bir_lowering=False, num_devices=1)
    aps = [nc.dram_tensor(name, a.shape, mybir.dt.from_np(a.dtype), kind="ExternalInput").ap()
           for name, a in arrays.items()]
    out = nc.dram_tensor("out_t", (P, KT, SEQ), F32, kind="ExternalOutput").ap()
    pairs = nc.dram_tensor("pairs_by_token", (HEADS, 2, SEQ, 2), F32, kind="Internal").ap()
    build(nc, *aps, pairs, out)
    r = run_bass_kernel_spmd(nc, [arrays], core_ids=[0])
    y = r.results[0]["out_t"]
    return np.ascontiguousarray(y.transpose(2, 1, 0).reshape(1, SEQ, D_MODEL))
```
